# Optimizing a Trainium2 kernel written in Bass

```python
import jax, jax.numpy as jnp
from jax import lax
import numpy as np

D_MODEL = 1024
BATCH = 1
SEQ = 1024
DEPTH = 1

HEAD_DIM = 64
ATTN_WIDTH = D_MODEL // 2
CONV_WIDTH = D_MODEL - ATTN_WIDTH
N_Q_HEADS = ATTN_WIDTH // HEAD_DIM
N_KV_HEADS = 2
GQA_GROUP = N_Q_HEADS // N_KV_HEADS
KV_WIDTH = N_KV_HEADS * HEAD_DIM
WINDOW = 128
BLOCK = 128
ROT_DIM = HEAD_DIM // 4
ROPE_THETA = 500000.0
CONV_W = 3
D_FF = 2816
N_MOD = 9
LN_EPS = 1e-5
DN_ALPHA = (2.0 * DEPTH) ** 0.25
DN_BETA = (8.0 * DEPTH) ** -0.25
IN_WIDTH = ATTN_WIDTH + 2 * KV_WIDTH + 3 * CONV_WIDTH

kernel_name = "hybrid_swa_sink_shortconv_macaron_deepnorm_adaln"

def layer_norm(x, g, b):
    xf = x.astype(jnp.float32)
    mu = jnp.mean(xf, axis=-1, keepdims=True)
    var = jnp.mean(jnp.square(xf - mu), axis=-1, keepdims=True)
    y = (xf - mu) * lax.rsqrt(var + LN_EPS) * g.astype(jnp.float32) + b.astype(jnp.float32)
    return y.astype(x.dtype)

def swiglu(h, w_gate_up, w_down):
    gu = h @ w_gate_up
    g, u = jnp.split(gu, 2, axis=-1)
    return (jax.nn.silu(g) * u) @ w_down

def partial_rope(x, positions):
    half = ROT_DIM // 2
    inv_freq = jnp.power(jnp.float32(ROPE_THETA), -jnp.arange(0, ROT_DIM, 2, dtype=jnp.float32) / ROT_DIM)
    ang = positions.astype(jnp.float32)[..., None] * inv_freq
    cos = jnp.cos(ang)[:, :, None, :].astype(x.dtype)
    sin = jnp.sin(ang)[:, :, None, :].astype(x.dtype)
    x1 = x[..., :half]
    x2 = x[..., half:ROT_DIM]
    rest = x[..., ROT_DIM:]
    return jnp.concatenate([x1 * cos - x2 * sin, x2 * cos + x1 * sin, rest], axis=-1)

def sliding_window_sink_attention(q, k, v, sinks):
    bsz, seq = q.shape[0], q.shape[1]
    nb = seq // BLOCK
    qb = q.reshape(bsz, nb, BLOCK, N_KV_HEADS, GQA_GROUP, HEAD_DIM)
    pad = ((0, 0), (BLOCK, 0), (0, 0), (0, 0))
    kp = jnp.pad(k, pad).reshape(bsz, nb + 1, BLOCK, N_KV_HEADS, HEAD_DIM)
    vp = jnp.pad(v, pad).reshape(bsz, nb + 1, BLOCK, N_KV_HEADS, HEAD_DIM)
    kb = jnp.concatenate([kp[:, :-1], kp[:, 1:]], axis=2)
    vb = jnp.concatenate([vp[:, :-1], vp[:, 1:]], axis=2)
    scale = HEAD_DIM ** -0.5
    scores = jnp.einsum('bnqhgd,bnkhd->bnhgqk', qb, kb).astype(jnp.float32) * scale
    blk = jnp.arange(nb)[:, None, None]
    qi = jnp.arange(BLOCK)[None, :, None]
    ki = jnp.arange(2 * BLOCK)[None, None, :]
    diff = qi + BLOCK - ki
    key_pos = (blk - 1) * BLOCK + ki
    valid = (diff >= 0) & (diff < WINDOW) & (key_pos >= 0)
    scores = jnp.where(valid[None, :, None, None], scores, -jnp.inf)
    sink = jnp.broadcast_to(
        sinks.astype(jnp.float32).reshape(N_KV_HEADS, GQA_GROUP)[None, None, :, :, None, None],
        scores.shape[:-1] + (1,))
    probs = jax.nn.softmax(jnp.concatenate([scores, sink], axis=-1), axis=-1)[..., :-1]
    out = jnp.einsum('bnhgqk,bnkhd->bnqhgd', probs.astype(v.dtype), vb)
    return out.reshape(bsz, seq, N_Q_HEADS * HEAD_DIM)

def short_gated_conv(u, b_gate, c_gate, conv_w):
    seq = u.shape[1]
    z = c_gate * u
    zp = jnp.pad(z, ((0, 0), (CONV_W - 1, 0), (0, 0)))
    y = conv_w[0] * zp[:, 0:seq]
    for tap in range(1, CONV_W):
        y = y + conv_w[tap] * zp[:, tap:tap + seq]
    return b_gate * y

def setup_inputs(seed: int = 0) -> dict:
    key = jax.random.key(seed)
    ks = jax.random.split(key, 20)
    nrm = lambda k, shape, s: jax.random.normal(k, shape, jnp.float32) * s
    L, D = DEPTH, D_MODEL
    x = jax.random.normal(ks[0], (BATCH, SEQ, D), jnp.float32)
    c = jax.random.normal(ks[1], (BATCH, D), jnp.float32)
    offsets = jax.random.randint(ks[2], (BATCH, 1), 0, 1024, dtype=jnp.int32)
    positions = offsets + jnp.arange(SEQ, dtype=jnp.int32)[None, :]
    return {
        "x": x,
        "c": c,
        "positions": positions,
        "w_ada": nrm(ks[3], (L, D, N_MOD * D), 0.1 * D ** -0.5),
        "b_ada": nrm(ks[4], (L, N_MOD * D), 0.01),
        "ffn1_w_gate_up": nrm(ks[5], (L, D, 2 * D_FF), D ** -0.5),
        "ffn1_w_down": nrm(ks[6], (L, D_FF, D), DN_BETA * D_FF ** -0.5),
        "ln1_g": 1.0 + nrm(ks[7], (L, D), 0.02),
        "ln1_b": nrm(ks[8], (L, D), 0.02),
        "w_in": nrm(ks[9], (L, D, IN_WIDTH), D ** -0.5),
        "conv_w": nrm(ks[10], (L, CONV_W, CONV_WIDTH), CONV_W ** -0.5),
        "attn_sinks": nrm(ks[11], (L, N_Q_HEADS), 1.0),
        "w_out": nrm(ks[12], (L, D, D), DN_BETA * D ** -0.5),
        "ln2_g": 1.0 + nrm(ks[13], (L, D), 0.02),
        "ln2_b": nrm(ks[14], (L, D), 0.02),
        "ffn2_w_gate_up": nrm(ks[15], (L, D, 2 * D_FF), D ** -0.5),
        "ffn2_w_down": nrm(ks[16], (L, D_FF, D), DN_BETA * D_FF ** -0.5),
        "ln3_g": 1.0 + nrm(ks[17], (L, D), 0.02),
        "ln3_b": nrm(ks[18], (L, D), 0.02),
    }

def reference(x, c, positions, w_ada, b_ada, ffn1_w_gate_up, ffn1_w_down, ln1_g, ln1_b,
              w_in, conv_w, attn_sinks, w_out, ln2_g, ln2_b,
              ffn2_w_gate_up, ffn2_w_down, ln3_g, ln3_b):
    bsz, seq = x.shape[0], x.shape[1]
    split_at = [ATTN_WIDTH, ATTN_WIDTH + KV_WIDTH, ATTN_WIDTH + 2 * KV_WIDTH,
                ATTN_WIDTH + 2 * KV_WIDTH + CONV_WIDTH, ATTN_WIDTH + 2 * KV_WIDTH + 2 * CONV_WIDTH]
    cond = jax.nn.silu(c)
    for l in range(DEPTH):
        mod = (cond @ w_ada[l] + b_ada[l])[:, None, :]
        sh1, sc1, g1, sh2, sc2, g2, sh3, sc3, g3 = jnp.split(mod, N_MOD, axis=-1)

        h = x * (1 + sc1) + sh1
        x = layer_norm(DN_ALPHA * x + 0.5 * (1 + g1) * swiglu(h, ffn1_w_gate_up[l], ffn1_w_down[l]),
                       ln1_g[l], ln1_b[l])

        h = x * (1 + sc2) + sh2
        proj = h @ w_in[l]
        q, k, v, u, b_gate, c_gate = jnp.split(proj, split_at, axis=-1)
        q = partial_rope(q.reshape(bsz, seq, N_Q_HEADS, HEAD_DIM), positions)
        k = partial_rope(k.reshape(bsz, seq, N_KV_HEADS, HEAD_DIM), positions)
        v = v.reshape(bsz, seq, N_KV_HEADS, HEAD_DIM)
        attn_out = sliding_window_sink_attention(q, k, v, attn_sinks[l])
        conv_out = short_gated_conv(u, b_gate, c_gate, conv_w[l])
        mix = jnp.concatenate([attn_out, conv_out], axis=-1) @ w_out[l]
        x = layer_norm(DN_ALPHA * x + (1 + g2) * mix, ln2_g[l], ln2_b[l])

        h = x * (1 + sc3) + sh3
        x = layer_norm(DN_ALPHA * x + 0.5 * (1 + g3) * swiglu(h, ffn2_w_gate_up[l], ffn2_w_down[l]),
                       ln3_g[l], ln3_b[l])
    return x


_drawn_inputs = setup_inputs


def setup_inputs(seed=0):
    import zlib

    import numpy as np

    out = dict(_drawn_inputs(seed))
    spreads = {}
    factors = {'b_ada': 5.093,
     'attn_sinks': 8.0,
     'ln2_g': 2.714,
     'ln2_b': 2.839,
     'ln3_g': 2.878,
     'ln3_b': 2.903}
    for name, (base, spread) in spreads.items():
        noise = np.random.default_rng([zlib.crc32(name.encode()), seed]).standard_normal(out[name].shape)
        drawn = base * np.exp(spread * noise) if base else spread * noise
        out[name] = __import__('jax').numpy.asarray(drawn.astype(out[name].dtype))
    for name, factor in factors.items():
        out[name] = (out[name] * factor).astype(out[name].dtype)
    return out
```

```python
from contextlib import ExitStack

import numpy as np

import concourse.bass as bass
import concourse.mybir as mybir
from concourse.alu_op_type import AluOpType as ALU

F32 = mybir.dt.float32
F32R = mybir.dt.float32r
I32 = mybir.dt.int32
ACT = mybir.ActivationFunctionType
AXX = mybir.AxisListType.X

P = 128
D = 1024
SEQ = 1024
KT = D // P
TT = SEQ // P
HALF = 512
D_FF = 2816
FC = D_FF // (2 * P)
HEAD_DIM = 64
N_HEADS = 8
PAIRS = N_HEADS // 2
ATTN_W = 512
CONV_W = 512
KV_W = 128
U0 = ATTN_W + 2 * KV_W
BG0 = U0 + CONV_W
CG0 = BG0 + CONV_W
ROT = 16
THETA = 500000.0
LN_EPS = 1e-5
ALPHA = 2.0 ** 0.25
SCALE = HEAD_DIM ** -0.5
MASKED = -1.0e30
N_MOD = 9
STRIPS = N_MOD * D // HALF
STRIPS_BEFORE = STRIPS - FC
PI = float(np.pi)

UNITS_FFN = 4 * FC
MIX0 = UNITS_FFN
FFN2_0 = MIX0 + 2 + 4 * PAIRS
CHUNK_MIX = FC
CHUNK_FFN2 = FC + PAIRS
PROD_MIX = 2 * FC
PROD_FFN2 = PROD_MIX + PAIRS

COL_C = 0
COL_LN = 8
COL_BADA = 40
COL_CONV = 112
N_COLS = 124

TWO_PI_1 = 6.28125
TWO_PI_2 = float(np.round((2 * np.pi - TWO_PI_1) * 2.0 ** 21) / 2.0 ** 21)
TWO_PI_3 = float(2 * np.pi - TWO_PI_1 - TWO_PI_2)
ROUND_1 = 1.5 * 2.0 ** 23
ROUND_2K = 1.5 * 2.0 ** 34


def unit(base, c, k):
    return base + 4 * c + k, base // 2 + 2 * c + k // 2, k % 2


def build(nc, t, out):
    with ExitStack() as ctx:
        def sb(name, shape, dt=F32):
            return ctx.enter_context(nc.sbuf_tensor(name, shape, dt))

        def sem(name):
            return ctx.enter_context(nc.semaphore(name))

        h_hi = sb("h_hi", [P, KT, SEQ], F32R)
        h_lo = sb("h_lo", [P, KT, SEQ], F32R)
        act_hi = sb("act_hi", [P, 2, SEQ], F32R)
        act_lo = sb("act_lo", [P, 2, SEQ], F32R)
        wu_hi = sb("wu_hi", [P, 2, D], F32R)
        wu_lo = sb("wu_lo", [P, 2, D], F32R)
        wd_hi = sb("wd_hi", [P, 2, D], F32R)
        wd_lo = sb("wd_lo", [P, 2, D], F32R)
        y = sb("y", [P, TT, D])
        raw_unit = sb("raw_unit", [P, 2, D])
        raw_down = sb("raw_down", [P, 2, D])
        arena = sb("arena", [P, 11, D])
        cos_t, sin_t, sg, prod, gate_row, k_t, v_tok, q_t, q_swap = (arena[:, i, :] for i in range(9))
        strip = arena[:, 7:11, :].rearrange("p a (b n) -> p (a b) n", n=HALF)
        scores = arena[:, 9, :].rearrange("p (s h k) -> p s h k", s=2, h=2)
        probsT = arena[:, 10, :].rearrange("p (s k h q) -> p s k h q", s=2, k=2, h=2)
        strip_acc = k_t[:, 0:HALF]
        h_tmp = v_tok.rearrange("p (s n) -> p s n", s=2)
        diag = v_tok
        const_rows = gate_row[0:N_COLS, 0:P]
        v_blk = v_tok.rearrange("p (b n) -> p b n", b=TT)
        ln_g_row, ln_b_row = arena[:, 9, :], arena[:, 10, :]
        out_g_row, out_b_row = q_t, q_swap
        mask = sb("mask", [P, 2 * P])
        ident = sb("ident", [P, P])
        ones = sb("ones", [P, P])
        rope_c = sb("rope_c", [P, 4])
        cols = sb("cols", [P, N_COLS])
        cond = sb("cond", [P, KT])
        mod = sb("mod", [P, 8 * N_MOD])
        affine = sb("affine", [P, 3, 2, KT])
        gate_c = sb("gate_c", [P, KT])
        sink = sb("sink", [P, 2, PAIRS])
        ln_s = sb("ln_s", [P, 2, 24])
        at_s = sb("at_s", [P, 2, 16])

        ps_unit = [ctx.enter_context(nc.psum_tensor(f"ps_unit{i}", [P, 2, HALF], F32)) for i in range(2)]
        ps_down = [ctx.enter_context(nc.psum_tensor(f"ps_down{i}", [P, 2, HALF], F32)) for i in range(2)]
        ps_mod = ps_down[1][:, 0, 0:4]
        ps_score = ps_down[0]
        ps_probsT = ps_down[1][:, 0, :].rearrange("p (k h q) -> p k h q", k=2, h=2)
        ps_attn = ps_down[1][:, 1, :]

        def flat(p):
            return p[:].rearrange("p a b -> p (a b)")

        s_const = sem("const_loaded")
        s_sink = sem("sink_loaded")
        s_x = [sem(f"x_loaded{i}") for i in range(2)]
        s_colsT = sem("cols_transposed")
        s_cols = sem("cols_copied")
        s_cond = sem("cond_ready")
        s_strip = [sem(f"strip_loaded{i}") for i in range(2)]
        s_acc = sem("strip_products")
        s_modmm = sem("mod_summed")
        s_mod = sem("mod_ready")
        s_aff = sem("affine_ready")
        s_diag = sem("gate_diagonal")
        s_gatemm = sem("gate_spread")
        s_gate = sem("gate_row_ready")
        s_rawu = [sem(f"unit_weights_loaded{i}") for i in range(2)]
        s_whi = sem("unit_weights_hi")
        s_wlo = sem("unit_weights_split")
        s_unit = sem("unit_done")
        s_pfree = [sem(f"unit_psum_read{i}") for i in range(2)]
        s_rawd = [sem(f"down_weights_loaded{i}") for i in range(2)]
        s_dgate = sem("down_weights_gated")
        s_dhi = sem("down_weights_hi")
        s_dlo = sem("down_weights_split")
        s_prod = sem("product_ready")
        s_phi = sem("product_hi")
        s_act = [sem(f"act_ready{i}") for i in range(2)]
        s_down = sem("down_tile_done")
        s_y = sem("y_added")
        s_ln = sem("ln_steps")
        s_var = sem("variance_ready")
        s_std = sem("deviation_ready")
        s_stat = sem("ln_scale_ready")
        s_norm = sem("rows_normalised")
        s_tr = sem("rows_transposed")
        s_ev = sem("h_affine_done")
        s_hhi = sem("h_hi_ready")
        s_h = sem("h_ready")
        s_rows = sem("ln_rows_loaded")
        s_rowsc = sem("ln_rows_scaled")
        s_rm = sem("residual_scaled")
        s_res = sem("residual_ready")
        s_pos = sem("positions_loaded")
        s_rt = sem("rope_table_steps")
        s_sin = sem("sines_ready")
        s_rtab = sem("rope_tables_ready")
        s_zero = sem("swap_zeroed")
        s_swap = sem("rotary_rows_swapped")
        s_rs = sem("rope_steps")
        s_rope = sem("rope_done")
        s_vT = sem("v_transposed")
        s_v = sem("v_ready")
        s_conv = sem("conv_steps")
        s_sc = sem("scores_ready")
        s_sm = sem("softmax_steps")
        s_msk = sem("scores_masked")
        s_max = sem("maximum_ready")
        s_exp = sem("exponentials_ready")
        s_p = sem("probs_ready")
        s_pT = sem("probs_transposed")
        s_pTc = sem("probsT_copied")
        s_pv = sem("values_summed")
        s_ahi = sem("attention_hi")
        s_alo = sem("attention_split")
        s_ow = sem("out_scaled")
        s_oa = sem("out_rows_ready")
        s_out = sem("out_stored")

        w_gu = [t["ffn1_w_gate_up"], t["ffn2_w_gate_up"]]
        w_dn = [t["ffn1_w_down"], t["ffn2_w_down"]]
        block = ctx.enter_context(nc.Block())

        @block.sync
        def _(sp):
            def wait_place(sem_, value):
                if not isinstance(value, int):
                    value = sp.to_reg(value)
                    sp.wait_ge(s_sink, 16)
                sp.wait_ge(sem_, value)

            def load_strip(n):
                for i in range(2):
                    free = None if isinstance(n, int) and n == 0 else sp.snap(8 * n - 4 + 4 * i)
                    src = t["w_ada"][HALF * i:HALF * (i + 1), bass.ds(HALF * n, HALF)]
                    if free is not None:
                        wait_place(s_acc, free)
                    sp.dma_start(strip[:, 4 * i:4 * i + 4, :], src.rearrange("(k p) n -> p k n", p=P)
                                 ).then_inc(s_strip[i], 16)

            def unit_columns(n, c, k):
                if isinstance(n, int) and MIX0 <= n < FFN2_0:
                    j, kind = divmod(n - MIX0 - 3, 4)
                    if n == MIX0:
                        col = ATTN_W + KV_W
                    elif n == MIX0 + 1:
                        col = ATTN_W
                    elif n == MIX0 + 2 or kind == 3:
                        j = 0 if n == MIX0 + 2 else j + 1
                        for h in range(2):
                            col = HEAD_DIM * (j + PAIRS * h)
                            yield (raw_unit[:, k % 2, :].rearrange("p (k h n) -> p h k n", k=KT, h=2)[:, h],
                                   t["w_in"][:, col:col + HEAD_DIM].rearrange("(k p) n -> p k n", p=P))
                        return
                    else:
                        col = (U0, CG0, BG0)[kind] + P * j
                    w = t["w_in"]
                else:
                    w = w_gu[0 if k is not None and c[0] == 0 else 1]
                    col = (0, D_FF, P, D_FF + P)[k] + 2 * P * c[1]
                for i in range(2):
                    yield (raw_unit[:, k % 2, HALF * i:HALF * (i + 1)].rearrange("p (k n) -> p k n", n=P),
                           w[HALF * i:HALF * (i + 1), bass.ds(col, P)].rearrange("(k p) n -> p k n", p=P))

            def load_unit(n, c, k):
                pieces = list(unit_columns(n, c, k))
                free = sp.snap(n - 1)
                wait_place(s_wlo, free)
                for dst, src in pieces:
                    sp.dma_start(dst, src).then_inc(s_rawu[k % 2], 16)

            def load_down(q, i, src0, src1):
                free = sp.snap(2 * q + i - 1)
                srcs = [w[bass.ds(r, 64), :] for w, r in (src0, src1)]
                wait_place(s_dlo, free)
                for m, src in enumerate(srcs):
                    sp.dma_start(raw_down[64 * m:64 * m + 64, i, :], src).then_inc(s_rawd[i], 16)

            def load_down_ffn(f, c):
                q = (0, CHUNK_FFN2)[f] + c
                for i in range(2):
                    r = 2 * P * c + P * i
                    load_down(q, i, (w_dn[f], r), (w_dn[f], r + 64))

            def load_down_mix(j):
                load_down(CHUNK_MIX + j, 0, (t["w_out"], HEAD_DIM * j), (t["w_out"], HEAD_DIM * (PAIRS + j)))
                load_down(CHUNK_MIX + j, 1, (t["w_out"], ATTN_W + P * j), (t["w_out"], ATTN_W + P * j + 64))

            def ffn_body(f, c, strip_n=None):
                base = (0, FFN2_0)[f]
                load_unit(base + 4 * c + 4, (f, c + 1), 0)
                if strip_n is not None:
                    load_strip(strip_n)
                load_down_ffn(f, c + 1)
                load_unit(base + 4 * c + 5, (f, c + 1), 1)
                load_unit(base + 4 * c + 6, (f, c + 1), 2)
                load_unit(base + 4 * c + 7, (f, c + 1), 3)

            for dst, src in ((const_rows[COL_C:COL_LN, :], t["c"].rearrange("a (r n) -> (a r) n", n=P)),
                             (const_rows[8:16, :], t["ln1_g"].rearrange("(r n) -> r n", n=P)),
                             (const_rows[16:24, :], t["ln1_b"].rearrange("(r n) -> r n", n=P)),
                             (const_rows[24:32, :], t["ln2_g"].rearrange("(r n) -> r n", n=P)),
                             (const_rows[32:40, :], t["ln2_b"].rearrange("(r n) -> r n", n=P)),
                             (const_rows[COL_BADA:COL_CONV, :], t["b_ada"].rearrange("(r n) -> r n", n=P)),
                             (const_rows[COL_CONV:N_COLS, :], t["conv_w"].rearrange("a (r n) -> (a r) n", n=P)),
                             (ident[:], t["ident"][:, :]), (ones[:], t["ones"][:, :]), (mask[:], t["mask"][:, :]),
                             (rope_c[:], t["rope_c"][:, :])):
                sp.dma_start(dst, src).then_inc(s_const, 16)
            sp.dma_start(sink[:].rearrange("p h j -> p (h j)"),
                         t["attn_sinks"].partition_broadcast(P)).then_inc(s_sink, 16)
            for n in range(4):
                load_strip(n)
            load_unit(2, (0, 0), 2)
            load_strip(4)
            load_strip(5)
            load_unit(3, (0, 0), 3)
            load_strip(6)
            ffn_body(0, 0, 7)
            with sp.Fori(1, FC - 1) as c:
                ffn_body(0, c, STRIPS_BEFORE + c)
            load_unit(MIX0, None, 0)
            load_strip(STRIPS - 1)
            load_down_mix(0)
            load_unit(MIX0 + 1, None, 1)
            sp.wait_ge(s_acc, 8 * STRIPS)
            sp.dma_start(q_t.bitcast(I32), t["positions"].partition_broadcast(P)).then_inc(s_pos, 16)
            sp.dma_start(ln_g_row, t["ln1_g"].partition_broadcast(P)).then_inc(s_rows, 16)
            sp.dma_start(ln_b_row, t["ln1_b"].partition_broadcast(P)).then_inc(s_rows, 16)
            load_unit(MIX0 + 2, None, 0)
            load_unit(MIX0 + 3, None, 1)
            for j in range(PAIRS):
                n = MIX0 + 4 * j + 4
                load_unit(n, None, 0)
                load_unit(n + 1, None, 1)
                if j + 1 < PAIRS:
                    load_unit(n + 2, None, 0)
                    load_down_mix(j + 1)
                    load_unit(n + 3, None, 1)
            load_unit(FFN2_0, (1, 0), 0)
            load_down_ffn(1, 0)
            load_unit(FFN2_0 + 1, (1, 0), 1)
            sp.wait_ge(s_pv, TT * PAIRS)
            sp.dma_start(ln_g_row, t["ln2_g"].partition_broadcast(P)).then_inc(s_rows, 16)
            sp.dma_start(ln_b_row, t["ln2_b"].partition_broadcast(P)).then_inc(s_rows, 16)
            sp.dma_start(out_g_row, t["ln3_g"].partition_broadcast(P)).then_inc(s_ow, 16)
            sp.dma_start(out_b_row, t["ln3_b"].partition_broadcast(P)).then_inc(s_ow, 16)
            load_unit(FFN2_0 + 2, (1, 0), 2)
            load_unit(FFN2_0 + 3, (1, 0), 3)
            ffn_body(1, 0)
            with sp.Fori(1, FC - 1) as c:
                ffn_body(1, c)
            for n in range(TT):
                sp.wait_ge(s_oa, n + 1)
                sp.dma_start(out[P * n:P * n + P, :], y[:, n, :]).then_inc(s_out, 16)
            sp.wait_ge(s_out, 16 * TT)

        @block.tensor
        def _(pe):
            def three(ps, st_hi, st_lo, mv_hi, mv_lo, first, last):
                n = len(ps)
                for i in range(n):
                    pe.matmul(ps[i], st_hi, mv_hi[i], start=first, stop=False)
                for i in range(n):
                    pe.matmul(ps[i], st_hi, mv_lo[i], start=False, stop=False)
                for i in range(n):
                    mm = pe.matmul(ps[i], st_lo, mv_hi[i], start=False, stop=last)
                return mm

            def halves(x):
                return [x[:, HALF * i:HALF * (i + 1)] for i in range(2)]

            def unit_kstep(par, k, parts=(0, 1)):
                w = slice(P * k, P * k + P)
                ps = [ps_unit[par][:, i, :] for i in parts]
                hi = [halves(h_hi[:, k, :])[i] for i in parts]
                lo = [halves(h_lo[:, k, :])[i] for i in parts]
                return three(ps, wu_hi[:, par, w], wu_lo[:, par, w], hi, lo, k == 0, k == KT - 1)

            def begin_unit(u):
                n, before, par = u
                pe.wait_ge(s_wlo, n + 1)
                if not (isinstance(before, int) and before == 0):
                    pe.wait_ge(s_pfree[par], before)

            def run_unit(u, beside=()):
                begin_unit(u)
                for k in range(KT):
                    mm = unit_kstep(u[2], k)
                    if k == KT - 1:
                        mm.then_inc(s_unit, 1)
                    if k < len(beside) and beside[k]:
                        beside[k]()

            def down_tile(q, n):
                if n == 0:
                    pe.wait_ge(s_dlo, 2 * q + 2)
                    pe.wait_ge(s_act[0], q + 1)
                    pe.wait_ge(s_act[1], q + 1)
                if not (isinstance(q, int) and q == 0 and n < 2):
                    pe.wait_ge(s_y, 8 * q + n - 1)
                ps = [ps_down[n % 2][:, i, :] for i in range(2)]
                tok = slice(P * n, P * n + P)
                seq = []
                for i in range(2):
                    for st, mv in ((act_hi, wd_hi), (act_hi, wd_lo), (act_lo, wd_hi)):
                        for h in range(2):
                            seq.append((h, st[:, i, tok], halves(mv[:, i, :])[h]))
                for m, (h, st, mv) in enumerate(seq):
                    mm = pe.matmul(ps[h], st, mv, start=m < 2, stop=m >= 10)
                    if m == 11:
                        mm.then_inc(s_down, 1)
                    if m % 3 == 2:
                        yield

            def down_all(q):
                for n in range(TT):
                    for _ in down_tile(q, n):
                        pass

            def transpose_rows(stage, half, d):
                if stage == 0:
                    pe.wait_ge(s_x[half], 64)
                else:
                    pe.wait_ge(s_norm, 8 * (stage - 1) + 4 * half + 4)
                n = 16 * stage + 8 * half + d
                if half == 0 and d == 0 and stage > 0:
                    pe.wait_ge(s_pfree[1], (0, MIX0 // 2, FFN2_0 // 2)[stage])
                if n >= 2:
                    pe.wait_ge(s_ev, n - 1)
                for i in range(4):
                    mm = pe.transpose(ps_unit[1][:, n % 2, P * i:P * i + P],
                                      y[:, 4 * half + i, P * d:P * d + P], ident[:])
                mm.then_inc(s_tr, 1)

            def first_unit(stage, base):
                begin_unit(unit(base, 0, 0))
                for k in range(KT):
                    pe.wait_ge(s_h, 16 * stage + k + 1)
                    unit_kstep(0, k, (0,))
                transpose_rows(stage, 1, 0)
                transpose_rows(stage, 1, 1)
                for k in range(KT):
                    pe.wait_ge(s_h, 16 * stage + 8 + k + 1)
                    mm = unit_kstep(0, k, (1,))
                    if k + 2 < KT:
                        transpose_rows(stage, 1, k + 2)
                mm.then_inc(s_unit, 1)
                pe.wait_ge(s_ev, 16 * (stage + 1))

            def down_and_turn(q, stage):
                for n in range(6):
                    for _ in down_tile(q, n):
                        pass
                for n in (6, 7):
                    for m, _ in enumerate(down_tile(q, n)):
                        transpose_rows(stage, 0, 4 * (n - 6) + m)

            def sum_strip(n, q=0):
                pe.wait_ge(s_acc, 8 * n + 8)
                if not isinstance(n, int) or n > 0:
                    pe.wait_ge(s_mod, n)
                if not isinstance(q, int) or q > 0:
                    pe.wait_ge(s_y, 8 * q)
                for i in range(4):
                    mm = pe.matmul(ps_mod[:, i:i + 1], strip_acc[:, P * i:P * i + P], ones[:, 0:1],
                                   start=True, stop=True)
                mm.then_inc(s_modmm, 1)

            def spread_gate(stage, q):
                pe.wait_ge(s_diag, stage + 1)
                if q > 0:
                    pe.wait_ge(s_y, 8 * q)
                for d in range(KT):
                    mm = pe.matmul(ps_down[0][:, d // 4, P * (d % 4):P * (d % 4) + P], ones[:],
                                   diag[:, P * d:P * d + P], start=True, stop=True)
                mm.then_inc(s_gatemm, 1)

            def ffn_body(f, c, strip_n=None, after_up=None, last=False):
                base, q0 = ((0, 0), (FFN2_0, CHUNK_FFN2))[f]
                run_unit(unit(base, c, 1))
                if after_up:
                    after_up()
                run_unit(unit(base, c, 2))
                run_unit(unit(base, c, 3))
                if not last:
                    run_unit(unit(base, c, 4))
                if strip_n is not None:
                    sum_strip(strip_n, q0 + c)
                    pe.wait_ge(s_mod, strip_n + 1)
                if not last:
                    down_all(q0 + c)

            pe.wait_ge(s_const, 16 * 11)
            pe.transpose(ps_unit[0][:, 0, 0:N_COLS], const_rows, ident[0:N_COLS, 0:N_COLS]
                         ).then_inc(s_colsT, 1)
            transpose_rows(0, 0, 0)
            transpose_rows(0, 0, 1)
            for n in range(4):
                sum_strip(n)
            for d in range(2, KT):
                transpose_rows(0, 0, d)
            pe.wait_ge(s_cols, 1)
            first_unit(0, 0)
            sum_strip(4)
            sum_strip(5)

            def first_gate():
                spread_gate(0, 0)
                sum_strip(6)
                pe.wait_ge(s_gate, 1)

            ffn_body(0, 0, 7, first_gate)
            with pe.Fori(1, FC - 1) as c:
                ffn_body(0, c, STRIPS_BEFORE + c)
            ffn_body(0, FC - 1, STRIPS - 1, last=True)
            down_and_turn(FC - 1, 1)

            first_unit(1, MIX0)
            run_unit(unit(MIX0, 0, 1))
            spread_gate(1, FC)
            pe.wait_ge(s_pfree[0], MIX0 // 2 + 1)
            pe.wait_ge(s_gate, 2)
            for b in range(TT):
                mm = pe.transpose(ps_down[0][:, b // 4, P * (b % 4):P * (b % 4) + P],
                                  sg[:, P * b:P * b + P], ident[:])
            mm.then_inc(s_vT, 1)
            run_unit(unit(MIX0, 0, 2))

            def score(j, b):
                n = TT * j + b
                if b == 0:
                    pe.wait_ge(s_rope, 2 + j)
                    pe.wait_ge(s_v, 1)
                    pe.wait_ge(s_y, 8 * (CHUNK_MIX + j))
                if n >= 1:
                    pe.wait_ge(s_msk, n)
                k0 = P * (b - 1) if b else 0
                for h in range(2):
                    r = slice(64 * h, 64 * h + 64)
                    o0 = 256 * (b % 2)
                    mm = pe.matmul(ps_score[:, h, o0 + (0 if b else P):o0 + 256], q_t[r, P * b:P * b + P],
                                   k_t[r, k0:P * b + P], start=True, stop=True)
                mm.then_inc(s_sc, 1)

            def turn_probs(j, b):
                n = TT * j + b
                pe.wait_ge(s_p, n + 1)
                if n >= 1:
                    pe.wait_ge(s_pTc, n)
                for k in range(0 if b else 1, 2):
                    for h in range(2):
                        mm = pe.transpose(ps_probsT[:, k, h, :], scores[:, b % 2, h, P * k:P * k + P],
                                          ident[:])
                mm.then_inc(s_pT, 1)

            def values(j, b):
                n = TT * j + b
                pe.wait_ge(s_pTc, n + 1)
                if b % 4 == 0 and n >= 4:
                    pe.wait_ge(s_alo, n // 4)
                for h in range(2):
                    for k in range(0 if b else 1, 2):
                        mm = pe.matmul(ps_attn[64 * h:64 * h + 64, P * (b % 4):P * (b % 4) + P],
                                       v_blk[:, b - 1 + k, 64 * h:64 * h + 64], probsT[:, b % 2, k, h, :],
                                       start=k == (0 if b else 1), stop=k == 1)
                mm.then_inc(s_pv, 1)

            for j in range(PAIRS):
                steps = [None] * 32
                for b in range(TT):
                    steps[3 * b] = lambda b=b: score(j, b)
                    steps[3 * b + 4] = lambda b=b: turn_probs(j, b)
                    steps[3 * b + 5] = lambda b=b: values(j, b)
                run_unit(unit(MIX0, j, 3), steps[0:8])
                run_unit(unit(MIX0, j, 4), steps[8:16])
                run_unit(unit(MIX0, j, 5), steps[16:24])
                if j + 1 < PAIRS:
                    run_unit(unit(MIX0, j, 6), steps[24:32])
                    down_all(CHUNK_MIX + j)
                else:
                    for s in steps[24:32]:
                        if s:
                            s()
            down_and_turn(CHUNK_MIX + PAIRS - 1, 2)

            first_unit(2, FFN2_0)
            ffn_body(1, 0, after_up=lambda: spread_gate(2, CHUNK_FFN2))
            with pe.Fori(1, FC - 1) as c:
                ffn_body(1, c)
            ffn_body(1, FC - 1, last=True)
            down_all(CHUNK_FFN2 + FC - 1)

        @block.scalar
        def _(act):
            def split_unit(u):
                n, before, par = u
                act.wait_ge(s_rawu[par], 32 * before + 32)
                if not (isinstance(n, int) and n < 2):
                    act.wait_ge(s_unit, n - 1)
                act.activation(wu_hi[:, par, :], raw_unit[:, par, :], ACT.Copy).then_inc(s_whi, 1)

            def split_down(q):
                for i in range(2):
                    act.wait_ge(s_dgate, 2 * q + i + 1)
                    if not (isinstance(q, int) and q == 0):
                        act.wait_ge(s_down, 8 * q)
                    act.activation(wd_hi[:, i, :], raw_down[:, i, :], ACT.Copy).then_inc(s_dhi, 1)

            def silu_gate(u):
                n, before, par = u
                act.wait_ge(s_unit, n + 1)
                if not (isinstance(before, int) and before == 0):
                    act.wait_ge(s_pfree[1], before)
                act.activation(sg, flat(ps_unit[par]), ACT.Silu).then_inc(s_pfree[par], 1)

            def product_hi(m, i, q):
                act.wait_ge(s_prod, m + 1)
                if not (isinstance(q, int) and q == 0):
                    act.wait_ge(s_down, 8 * q)
                act.activation(act_hi[:, i, :], prod, ACT.Copy).then_inc(s_phi, 1)

            def h_out(stage, half, d):
                n = 16 * stage + 8 * half + d
                act.wait_ge(s_tr, n + 1)
                act.wait_ge(s_aff, stage + 1)
                if n >= 2:
                    act.wait_ge(s_h, n - 1)
                act.activation(h_tmp[:, n % 2, :], ps_unit[1][:, n % 2, :], ACT.Identity,
                               bias=affine[:, stage, 1, d:d + 1], scale=affine[:, stage, 0, d:d + 1]
                               ).then_inc(s_ev, 1)

            def deviation(ln, n):
                m = TT * ln + n
                act.wait_ge(s_var, m + 1)
                act.activation(ln_s[:, n % 2, 15:16], ln_s[:, n % 2, 14:15], ACT.Sqrt).then_inc(s_std, 1)

            def normalise(ln, n):
                m = TT * ln + n
                act.wait_ge(s_stat, m + 1)
                act.activation(y[:, n, :], y[:, n, :], ACT.Identity, bias=ln_s[:, n % 2, 21:22],
                               scale=ln_s[:, n % 2, 20:21]).then_inc(s_norm, 1)

            def ln_turn(stage):
                for n in range(6):
                    deviation(stage - 1, n)
                    normalise(stage - 1, n)
                for d in range(KT):
                    h_out(stage, 0, d)
                for n in (6, 7):
                    deviation(stage - 1, n)
                    normalise(stage - 1, n)
                for d in range(KT):
                    h_out(stage, 1, d)

            def ffn_body(f, c, last=False):
                base, q0, m0 = ((0, 0, 0), (FFN2_0, CHUNK_FFN2, PROD_FFN2))[f]
                split_unit(unit(base, c, 2))
                split_down(q0 + c)
                split_unit(unit(base, c, 3))
                product_hi(m0 + 2 * c, 0, q0 + c)
                silu_gate(unit(base, c, 2))
                if not (last and f):
                    split_unit(unit(base, c, 4))
                    split_unit(unit(base, c, 5))
                product_hi(m0 + 2 * c + 1, 1, q0 + c)
                if not last:
                    silu_gate(unit(base, c, 4))

            def gate_out(stage):
                act.wait_ge(s_gatemm, stage + 1)
                q = (0, CHUNK_MIX, CHUNK_FFN2)[stage]
                if q:
                    act.wait_ge(s_dgate, 2 * q)
                act.activation(gate_row, flat(ps_down[0]), ACT.Copy).then_inc(s_gate, 1)

            for n in range(TT):
                act.dma_start(y[:, n, :], t["x"][P * n:P * n + P, :]).then_inc(s_x[n // 4], 16)
            for k in range(2):
                for i in range(2):
                    act.dma_start(raw_unit[:, k, HALF * i:HALF * (i + 1)].rearrange("p (k n) -> p k n", n=P),
                                  w_gu[0][HALF * i:HALF * (i + 1), D_FF * k:D_FF * k + P]
                                  .rearrange("(k p) n -> p k n", p=P)).then_inc(s_rawu[k], 16)
            for i in range(2):
                for m in range(2):
                    r = P * i + 64 * m
                    act.dma_start(raw_down[64 * m:64 * m + 64, i, :], w_dn[0][r:r + 64, :]
                                  ).then_inc(s_rawd[i], 16)
            act.wait_ge(s_cols, 1)
            act.activation(cond[:], cols[:, COL_C:COL_C + KT], ACT.Silu).then_inc(s_cond, 1)
            split_unit(unit(0, 0, 0))
            split_unit(unit(0, 0, 1))
            for half in range(2):
                for d in range(KT):
                    h_out(0, half, d)
            silu_gate(unit(0, 0, 0))
            gate_out(0)
            ffn_body(0, 0)
            with act.Fori(1, FC - 1) as c:
                ffn_body(0, c)
            ffn_body(0, FC - 1, last=True)
            act.wait_ge(s_rtab, 1)
            act.activation(sin_t, sin_t, ACT.Sin).then_inc(s_sin, 1)
            act.activation(cos_t, cos_t, ACT.Sin).then_inc(s_sin, 1)
            ln_turn(1)

            def copy_out(dst, u):
                n, before, par = u
                act.wait_ge(s_unit, n + 1)
                act.activation(dst, flat(ps_unit[par]), ACT.Copy).then_inc(s_pfree[par], 1)

            def swap_rotary(src, r):
                act.wait_ge(s_zero, 1)
                if r > 0:
                    act.wait_ge(s_rope, r)
                for b in (0, 64):
                    act.dma_start(q_swap[b:b + 8, :], src[b + 8:b + 16, :]).then_inc(s_swap, 16)
                    act.dma_start(q_swap[b + 8:b + 16, :], src[b:b + 8, :]).then_inc(s_swap, 16)

            split_unit(unit(MIX0, 0, 2))
            act.wait_ge(s_prod, PROD_MIX)
            copy_out(sg, unit(MIX0, 0, 0))
            copy_out(k_t, unit(MIX0, 0, 1))
            act.wait_ge(s_pfree[1], MIX0 // 2 + 1)
            swap_rotary(k_t, 0)
            split_unit(unit(MIX0, 0, 3))
            gate_out(1)
            act.wait_ge(s_vT, 1)
            act.activation(v_tok, flat(ps_down[0]), ACT.Copy).then_inc(s_v, 1)
            split_down(CHUNK_MIX)
            copy_out(q_t, unit(MIX0, 0, 2))
            act.wait_ge(s_pfree[0], MIX0 // 2 + 2)
            swap_rotary(q_t, 1)

            def exps(j, b):
                n = TT * j + b
                k0 = 0 if b else P
                act.wait_ge(s_max, n + 1)
                for h in range(2):
                    act.activation(scores[:, b % 2, h, k0:], scores[:, b % 2, h, k0:], ACT.Exp,
                                   bias=at_s[:, b % 2, 2 + h:3 + h],
                                   accum_out=at_s[:, b % 2, 6 + h:7 + h])
                act.activation(at_s[:, b % 2, 8:10], at_s[:, b % 2, 4:6], ACT.Exp).then_inc(s_exp, 1)

            def probsT_out(j, b):
                n = TT * j + b
                act.wait_ge(s_pT, n + 1)
                if n >= 2:
                    act.wait_ge(s_pv, n - 1)
                k0 = 0 if b else 1
                act.activation(probsT[:, b % 2, k0:], ps_probsT[:, k0:], ACT.Copy).then_inc(s_pTc, 1)

            def attn_hi(j, g):
                act.wait_ge(s_pv, TT * j + 4 * g + 4)
                act.wait_ge(s_down, 8 * (CHUNK_MIX + j))
                act.activation(act_hi[:, 0, HALF * g:HALF * (g + 1)], ps_attn, ACT.Copy).then_inc(s_ahi, 1)

            for j in range(PAIRS):
                last = j + 1 == PAIRS
                exps(j, 0)
                exps(j, 1)
                probsT_out(j, 0)
                split_unit(unit(MIX0, j, 4))
                exps(j, 2)
                probsT_out(j, 1)
                act.wait_ge(s_prod, PROD_MIX + j)
                copy_out(sg, unit(MIX0, j, 3))
                split_unit(unit(MIX0, j, 5))
                exps(j, 3)
                probsT_out(j, 2)
                exps(j, 4)
                probsT_out(j, 3)
                attn_hi(j, 0)
                exps(j, 5)
                probsT_out(j, 4)
                if not last:
                    split_unit(unit(MIX0, j, 6))
                else:
                    split_unit(unit(FFN2_0, 0, 0))
                exps(j, 6)
                probsT_out(j, 5)
                exps(j, 7)
                probsT_out(j, 6)
                probsT_out(j, 7)
                product_hi(PROD_MIX + j, 1, CHUNK_MIX + j)
                split_unit(unit(MIX0, j, 7) if not last else unit(FFN2_0, 0, 1))
                attn_hi(j, 1)
                if not last:
                    copy_out(q_t, unit(MIX0, j, 6))
                    act.wait_ge(s_pfree[0], MIX0 // 2 + 4 + 2 * j)
                    swap_rotary(q_t, 2 + j)
                    split_down(CHUNK_MIX + j + 1)
            ln_turn(2)

            silu_gate(unit(FFN2_0, 0, 0))
            gate_out(2)
            ffn_body(1, 0)
            with act.Fori(1, FC - 1) as c:
                ffn_body(1, c)
            ffn_body(1, FC - 1, last=True)
            for n in range(TT):
                deviation(2, n)
                normalise(2, n)

        @block.vector
        def _(dve):
            def split_unit(u):
                n, before, par = u
                dve.wait_ge(s_whi, n + 1)
                dve.tensor_tensor(wu_lo[:, par, :], raw_unit[:, par, :], wu_hi[:, par, :].bitcast(F32),
                                  ALU.subtract).then_inc(s_wlo, 1)

            def split_down(q):
                for i in range(2):
                    dve.wait_ge(s_dhi, 2 * q + i + 1)
                    dve.tensor_tensor(wd_lo[:, i, :], raw_down[:, i, :], wd_hi[:, i, :].bitcast(F32),
                                      ALU.subtract).then_inc(s_dlo, 1)

            def glu(u, m, i, q):
                n, before, par = u
                dve.wait_ge(s_unit, n + 1)
                dve.wait_ge(s_pfree[0], before + 1)
                if not (isinstance(q, int) and q == 0 and i == 0):
                    dve.wait_ge(s_act[1 - i], q + i)
                dve.tensor_tensor(prod, sg, flat(ps_unit[par]), ALU.mult).then_inc(s_pfree[par], 1)

            def product_lo(m, i):
                dve.wait_ge(s_phi, m + 1)
                dve.tensor_tensor(act_lo[:, i, :], prod, act_hi[:, i, :].bitcast(F32),
                                  ALU.subtract).then_inc(s_act[i], 1)

            def strip_products(n):
                for k in range(KT):
                    if k % 4 == 0:
                        dve.wait_ge(s_strip[k // 4], 16 * n + 16)
                    if k == 0:
                        if not (isinstance(n, int) and n == 0):
                            dve.wait_ge(s_modmm, n)
                        dve.tensor_scalar(strip_acc, strip[:, 0, :], cond[:, 0:1], None, ALU.mult
                                          ).then_inc(s_acc, 1)
                        continue
                    dve.wait_ge(s_acc, 8 * n + k)
                    dve.scalar_tensor_tensor(strip_acc, strip[:, k, :], cond[:, k:k + 1], strip_acc,
                                             ALU.mult, ALU.add).then_inc(s_acc, 1)

            def mod_out(n):
                dve.wait_ge(s_modmm, n + 1)
                dve.tensor_tensor(mod[:, bass.ds(4 * n, 4)], ps_mod, cols[:, bass.ds(COL_BADA + 4 * n, 4)],
                                  ALU.add).then_inc(s_mod, 1)

            def affine_cols(stage):
                sh, sc = mod[:, 24 * stage:24 * stage + 8], mod[:, 24 * stage + 8:24 * stage + 16]
                a, b = affine[:, stage, 0, :], affine[:, stage, 1, :]
                if stage == 0:
                    dve.tensor_scalar(a, sc, 1.0, None, ALU.add).then_inc(s_ln, 1)
                    dve.tensor_scalar(b, sh, 0.0, None, ALU.add).then_inc(s_ln, 1)
                    dve.wait_ge(s_ln, steps(2))
                    dve.nop().then_inc(s_aff, 1)
                    return
                g = cols[:, COL_LN + 16 * (stage - 1):COL_LN + 16 * (stage - 1) + 8]
                lb = cols[:, COL_LN + 16 * (stage - 1) + 8:COL_LN + 16 * stage]
                dve.scalar_tensor_tensor(a, sc, 1.0, g, ALU.add, ALU.mult).then_inc(s_ln, 1)
                dve.scalar_tensor_tensor(b, sc, 1.0, lb, ALU.add, ALU.mult).then_inc(s_ln, 1)
                dve.wait_ge(s_ln, steps(2))
                dve.tensor_tensor(b, b, sh, ALU.add).then_inc(s_aff, 1)

            ln_count = [0]

            def steps(n):
                ln_count[0] += n
                return ln_count[0]

            def gate_diagonal(stage):
                g = mod[:, 24 * stage + 16:24 * stage + 24]
                factor = (0.5, 1.0, 0.5)[stage]
                dve.tensor_scalar(gate_c[:], g, 1.0, factor, ALU.add, ALU.mult).then_inc(s_ln, 1)
                dve.wait_ge(s_ln, steps(1))
                dve.wait_ge(s_h, 16 * (stage + 1))
                for d in range(KT):
                    ins = dve.tensor_scalar(diag[:, P * d:P * d + P], ident[:], gate_c[:, d:d + 1], None,
                                            ALU.mult)
                ins.then_inc(s_diag, 1)

            def h_split(stage, half, d):
                n = 16 * stage + 8 * half + d
                dve.wait_ge(s_hhi, n + 1)
                at = slice(HALF * half, HALF * half + HALF)
                dve.tensor_tensor(h_lo[:, d, at], h_tmp[:, n % 2, :], h_hi[:, d, at].bitcast(F32),
                                  ALU.subtract).then_inc(s_h, 1)

            def add_y(q, n, stage=None):
                dve.wait_ge(s_down, 8 * q + n + 1)
                if stage is not None:
                    dve.wait_ge(s_res, 8 * stage + n + 1)
                elif not (isinstance(q, int) and q == 0):
                    dve.wait_ge(s_y, 8 * q + n - 7)
                dve.tensor_tensor(y[:, n, :], y[:, n, :], flat(ps_down[n % 2]), ALU.add).then_inc(s_y, 1)

            def statistics(ln, q, n):
                s = ln_s[:, n % 2, :]
                m = TT * ln + n
                add_y(q, n)
                if m >= 2:
                    dve.wait_ge(s_norm, m - 1)
                dve.wait_ge(s_y, 8 * q + n + 1)
                for i in range(2):
                    dve.bn_stats(s[:, 6 * i:6 * i + 6], y[:, n, HALF * i:HALF * i + HALF]).then_inc(s_ln, 1)
                dve.wait_ge(s_ln, steps(2))
                dve.bn_aggr(s[:, 12:14], s[:, 0:12]).then_inc(s_ln, 1)
                dve.wait_ge(s_ln, steps(1))
                dve.tensor_scalar(s[:, 14:15], s[:, 13:14], LN_EPS, None, ALU.add).then_inc(s_var, 1)

            def row_scale(ln, n):
                s = ln_s[:, n % 2, :]
                m = TT * ln + n
                dve.wait_ge(s_std, m + 1)
                dve.reciprocal(s[:, 16:17], s[:, 15:16]).then_inc(s_ln, 1)
                dve.wait_ge(s_ln, steps(1))
                dve.scalar_tensor_tensor(s[:, 17:18], s[:, 16:17], s[:, 14:15], s[:, 16:17], ALU.mult,
                                         ALU.mult).then_inc(s_ln, 1)
                dve.wait_ge(s_ln, steps(1))
                dve.tensor_scalar(s[:, 18:19], s[:, 17:18], -0.5, 1.5, ALU.mult, ALU.add).then_inc(s_ln, 1)
                dve.wait_ge(s_ln, steps(1))
                dve.tensor_tensor(s[:, 20:21], s[:, 16:17], s[:, 18:19], ALU.mult).then_inc(s_ln, 1)
                dve.wait_ge(s_ln, steps(1))
                dve.scalar_tensor_tensor(s[:, 21:22], s[:, 12:13], -1.0, s[:, 20:21], ALU.mult, ALU.mult
                                         ).then_inc(s_stat, 1)

            def ln_turn(stage, q):
                ln = stage - 1
                for n in range(6):
                    statistics(ln, q, n)
                    row_scale(ln, n)
                for d in range(4):
                    h_split(stage, 0, d)
                statistics(ln, q, 6)
                for d in range(4, KT):
                    h_split(stage, 0, d)
                statistics(ln, q, 7)
                row_scale(ln, 6)
                row_scale(ln, 7)
                for d in range(KT):
                    h_split(stage, 1, d)

            def ffn_body(f, c, strip_n=None, first=False, last=False, between=None):
                base, q0, m0 = ((0, 0, 0), (FFN2_0, CHUNK_FFN2, PROD_FFN2))[f]
                split_unit(unit(base, c, 2))
                split_down(q0 + c)
                glu(unit(base, c, 1), m0 + 2 * c, 0, q0 + c)
                dve.wait_ge(s_pfree[1], base // 2 + 2 * c + 1)
                dve.nop().then_inc(s_prod, 1)
                split_unit(unit(base, c, 3))
                product_lo(m0 + 2 * c, 0)
                if strip_n is not None:
                    strip_products(strip_n)
                if between:
                    between()
                if not (last and f):
                    split_unit(unit(base, c, 4))
                glu(unit(base, c, 3), m0 + 2 * c + 1, 1, q0 + c)
                dve.wait_ge(s_pfree[1], base // 2 + 2 * c + 2)
                dve.nop().then_inc(s_prod, 1)
                if not (last and f):
                    split_unit(unit(base, c, 5))
                product_lo(m0 + 2 * c + 1, 1)
                if strip_n is not None:
                    mod_out(strip_n)
                if not last:
                    for n in range(TT):
                        add_y(q0 + c, n, 2 * f if first else None)

            dve.wait_ge(s_colsT, 1)
            dve.tensor_copy(cols[:], ps_unit[0][:, 0, 0:N_COLS]).then_inc(s_cols, 1)
            dve.wait_ge(s_cond, 1)
            strip_products(0)
            for n in range(1, 4):
                mod_out(n - 1)
                strip_products(n)
            mod_out(3)
            dve.wait_ge(s_mod, 4)
            affine_cols(0)
            split_unit(unit(0, 0, 0))
            for d in range(KT):
                h_split(0, 0, d)
            split_unit(unit(0, 0, 1))
            for d in range(KT):
                h_split(0, 1, d)
            for n in (4, 5):
                strip_products(n)
                mod_out(n)
            dve.wait_ge(s_mod, 6)
            gate_diagonal(0)
            strip_products(6)
            mod_out(6)
            ffn_body(0, 0, 7, first=True)
            with dve.Fori(1, FC - 1) as c:
                ffn_body(0, c, STRIPS_BEFORE + c)

            def rope_tables():
                done = [0]

                def step(ins):
                    ins.then_inc(s_rt, 1)
                    done[0] += 1
                    dve.wait_ge(s_rt, done[0])
                tmp, ang, turns = q_swap, cos_t, sin_t
                dve.wait_ge(s_pos, 16)
                step(dve.tensor_copy(tmp, q_t.bitcast(I32)))
                step(dve.tensor_scalar(ang, tmp, rope_c[:, 0:1], None, ALU.mult))
                step(dve.tensor_scalar(turns, ang, 1.0 / (2 * PI), None, ALU.mult))
                step(dve.tensor_scalar(turns, turns, ROUND_1, None, ALU.add))
                step(dve.tensor_scalar(turns, turns, -ROUND_1, None, ALU.add))
                step(dve.tensor_scalar(tmp, turns, ROUND_2K, None, ALU.add))
                step(dve.tensor_scalar(tmp, tmp, -ROUND_2K, None, ALU.add))
                step(dve.tensor_tensor(turns, turns, tmp, ALU.subtract))
                for part in (TWO_PI_1, TWO_PI_2, TWO_PI_3):
                    for n in (tmp, turns):
                        step(dve.scalar_tensor_tensor(ang, n, -part, ang, ALU.mult, ALU.add))
                step(dve.tensor_scalar(turns, ang, PI, -PI, ALU.min, ALU.max))
                step(dve.tensor_scalar(ang, ang, PI / 2, None, ALU.add))
                step(dve.tensor_scalar(tmp, ang, PI, -2 * PI, ALU.is_gt, ALU.mult))
                step(dve.tensor_tensor(ang, ang, tmp, ALU.add))
                step(dve.tensor_scalar(cos_t, ang, PI, -PI, ALU.min, ALU.max))
                dve.nop().then_inc(s_rtab, 1)

            ffn_body(0, FC - 1, STRIPS - 1, last=True, between=rope_tables)
            dve.wait_ge(s_mod, STRIPS)
            affine_cols(1)
            affine_cols(2)
            dve.wait_ge(s_sin, 2)
            dve.tensor_scalar(sin_t, sin_t, rope_c[:, 1:2], None, ALU.mult).then_inc(s_rtab, 1)
            dve.tensor_scalar(cos_t, cos_t, rope_c[:, 2:3], rope_c[:, 3:4], ALU.mult, ALU.add
                              ).then_inc(s_rtab, 1)
            ln_turn(1, FC - 1)

            gate_diagonal(1)
            split_unit(unit(MIX0, 0, 2))
            rope_n = [0]

            def rope(dst, r):
                dve.wait_ge(s_swap, 64 * (r + 1))
                dve.tensor_tensor(q_swap, q_swap, sin_t, ALU.mult).then_inc(s_rs, 1)
                dve.tensor_tensor(dst, dst, cos_t, ALU.mult).then_inc(s_rs, 1)
                dve.wait_ge(s_rs, 2 * (r + 1))
                dve.tensor_tensor(dst, dst, q_swap, ALU.add).then_inc(s_rope, 1)

            dve.wait_ge(s_rtab, 3)
            rope(k_t, 0)
            split_unit(unit(MIX0, 0, 3))
            split_down(CHUNK_MIX)
            rope(q_t, 1)
            sm = [0]

            def sm_step():
                sm[0] += 1
                return sm[0]

            def softmax_max(j, b):
                n = TT * j + b
                k0 = 0 if b else P
                s = at_s[:, b % 2, :]
                dve.wait_ge(s_sc, n + 1)
                if n >= 2:
                    dve.wait_ge(s_pT, n - 1)
                sc = scores[:, b % 2, :, k0:]
                ps = ps_score[:, :, 256 * (b % 2) + k0:256 * (b % 2) + 256]
                mk = mask[:, k0:].unsqueeze(1).to_broadcast([P, 2, 2 * P - k0])
                dve.scalar_tensor_tensor(sc, ps, SCALE, mk, ALU.mult, ALU.add).then_inc(s_msk, 1)
                dve.wait_ge(s_msk, n + 1)
                dve.tensor_reduce(s[:, 0:2], sc, AXX, ALU.max).then_inc(s_sm, 1)
                dve.wait_ge(s_sm, sm_step())
                dve.tensor_tensor(s[:, 0:2], s[:, 0:2], sink[:, :, j], ALU.max).then_inc(s_sm, 1)
                dve.wait_ge(s_sm, sm_step())
                dve.tensor_scalar(s[:, 2:4], s[:, 0:2], -1.0, None, ALU.mult).then_inc(s_sm, 1)
                dve.wait_ge(s_sm, sm_step())
                dve.tensor_tensor(s[:, 4:6], sink[:, :, j], s[:, 2:4], ALU.add).then_inc(s_max, 1)

            def softmax_norm(j, b):
                n = TT * j + b
                k0 = 0 if b else P
                s = at_s[:, b % 2, :]
                dve.wait_ge(s_exp, n + 1)
                dve.tensor_tensor(s[:, 10:12], s[:, 6:8], s[:, 8:10], ALU.add).then_inc(s_sm, 1)
                dve.wait_ge(s_sm, sm_step())
                dve.reciprocal(s[:, 12:14], s[:, 10:12]).then_inc(s_sm, 1)
                dve.wait_ge(s_sm, sm_step())
                sc = scores[:, b % 2, :, k0:]
                dve.tensor_tensor(sc, sc, s[:, 12:14].unsqueeze(2).to_broadcast([P, 2, 2 * P - k0]),
                                  ALU.mult).then_inc(s_p, 1)

            def attn_lo(j, g):
                dve.wait_ge(s_ahi, 2 * j + g + 1)
                at = slice(HALF * g, HALF * g + HALF)
                dve.tensor_tensor(act_lo[:, 0, at], ps_attn, act_hi[:, 0, at].bitcast(F32), ALU.subtract
                                  ).then_inc(s_alo, 1)
                if g == 1:
                    dve.wait_ge(s_alo, 2 * j + 2)
                    dve.nop().then_inc(s_act[0], 1)

            def conv(j):
                w = [cols[:, COL_CONV + 4 * tap + j:COL_CONV + 4 * tap + j + 1] for tap in range(3)]
                dve.wait_ge(s_unit, MIX0 + 4 * j + 5)
                dve.wait_ge(s_pfree[1], MIX0 // 2 + 2 * j + 2)
                dve.tensor_tensor(sg, sg, flat(ps_unit[0]), ALU.mult).then_inc(s_pfree[0], 1)
                dve.wait_ge(s_pfree[0], MIX0 // 2 + 2 * j + 3)
                dve.wait_ge(s_act[1], CHUNK_MIX + j)
                dve.tensor_scalar(prod, sg, w[2], None, ALU.mult).then_inc(s_conv, 1)
                for tap in (1, 0):
                    lag = 2 - tap
                    dve.wait_ge(s_conv, 3 * j + lag)
                    dve.scalar_tensor_tensor(prod[:, lag:], sg[:, 0:SEQ - lag], w[tap], prod[:, lag:],
                                             ALU.mult, ALU.add).then_inc(s_conv, 1)
                dve.wait_ge(s_conv, 3 * j + 3)

            def conv_gate(j):
                dve.wait_ge(s_unit, MIX0 + 4 * j + 6)
                dve.tensor_tensor(prod, prod, flat(ps_unit[1]), ALU.mult).then_inc(s_pfree[1], 1)
                dve.wait_ge(s_pfree[1], MIX0 // 2 + 2 * j + 3)
                dve.nop().then_inc(s_prod, 1)

            for j in range(PAIRS):
                last = j + 1 == PAIRS
                softmax_max(j, 0)
                softmax_max(j, 1)
                softmax_norm(j, 0)
                split_unit(unit(MIX0, j, 4))
                softmax_max(j, 2)
                softmax_norm(j, 1)
                split_unit(unit(MIX0, j, 5))
                softmax_max(j, 3)
                softmax_norm(j, 2)
                softmax_max(j, 4)
                softmax_norm(j, 3)
                attn_lo(j, 0)
                softmax_max(j, 5)
                softmax_norm(j, 4)
                conv(j)
                split_unit(unit(MIX0, j, 6) if not last else unit(FFN2_0, 0, 0))
                softmax_max(j, 6)
                softmax_norm(j, 5)
                softmax_max(j, 7)
                softmax_norm(j, 6)
                softmax_norm(j, 7)
                conv_gate(j)
                product_lo(PROD_MIX + j, 1)
                split_unit(unit(MIX0, j, 7) if not last else unit(FFN2_0, 0, 1))
                attn_lo(j, 1)
                if not last:
                    for n in range(4):
                        add_y(CHUNK_MIX + j, n, 1 if j == 0 else None)
                    rope(q_t, 2 + j)
                    for n in range(4, TT):
                        add_y(CHUNK_MIX + j, n, 1 if j == 0 else None)
                    split_down(CHUNK_MIX + j + 1)
            ln_turn(2, CHUNK_MIX + PAIRS - 1)

            gate_diagonal(2)
            ffn_body(1, 0, first=True)
            with dve.Fori(1, FC - 1) as c:
                ffn_body(1, c)
            ffn_body(1, FC - 1, last=True)
            dve.wait_ge(s_ow, 32)
            for n in range(TT + 1):
                if n < TT:
                    statistics(2, CHUNK_FFN2 + FC - 1, n)
                    row_scale(2, n)
                if n > 0:
                    dve.wait_ge(s_norm, 16 + n)
                    dve.tensor_tensor(y[:, n - 1, :], y[:, n - 1, :], out_g_row, ALU.mult).then_inc(s_rt, 1)

        @block.gpsimd
        def _(pool):
            def gate_down(q):
                for i in range(2):
                    pool.wait_ge(s_rawd[i], 32 * q + 32)
                    pool.tensor_tensor(raw_down[:, i, :], raw_down[:, i, :], gate_row, ALU.mult
                                       ).then_inc(s_dgate, 1)

            def h_high(stage, half, d):
                n = 16 * stage + 8 * half + d
                pool.wait_ge(s_ev, n + 1)
                pool.tensor_copy(h_hi[:, d, HALF * half:HALF * half + HALF], h_tmp[:, n % 2, :]
                                 ).then_inc(s_hhi, 1)

            def residual(stage, n):
                pool.wait_ge(s_tr, 16 * stage + 8 * (n // 4) + 8)
                if stage == 0:
                    pool.tensor_scalar(y[:, n, :], y[:, n, :], ALPHA, None, ALU.mult).then_inc(s_res, 1)
                    return
                pool.tensor_tensor(y[:, n, :], y[:, n, :], ln_g_row, ALU.mult).then_inc(s_rm, 1)
                pool.wait_ge(s_rm, 8 * (stage - 1) + n + 1)
                pool.tensor_tensor(y[:, n, :], y[:, n, :], ln_b_row, ALU.add).then_inc(s_res, 1)

            def scale_rows(stage):
                pool.wait_ge(s_rows, 32 * stage)
                for m, row in enumerate((ln_g_row, ln_b_row)):
                    pool.tensor_scalar(row, row, ALPHA, None, ALU.mult).then_inc(s_rowsc, 1)
                pool.wait_ge(s_rowsc, 2 * stage)

            for half in range(2):
                for d in range(KT):
                    h_high(0, half, d)
            for n in range(TT):
                residual(0, n)
            pool.wait_ge(s_gate, 1)
            gate_down(0)
            with pool.Fori(1, FC) as c:
                gate_down(c)
            for stage, q in ((1, CHUNK_MIX), (2, CHUNK_FFN2)):
                scale_rows(stage)
                pool.wait_ge(s_unit, (0, MIX0, FFN2_0)[stage])
                for half in range(2):
                    for d in range(KT):
                        h_high(stage, half, d)
                if stage == 1:
                    pool.wait_ge(s_rt, 19)
                    pool.memset(q_swap, 0.0).then_inc(s_zero, 1)
                for n in range(TT):
                    residual(stage, n)
                pool.wait_ge(s_gate, stage + 1)
                gate_down(q)
                if stage == 1:
                    for j in range(1, PAIRS):
                        gate_down(q + j)
            with pool.Fori(1, FC) as c:
                gate_down(CHUNK_FFN2 + c)
            for n in range(TT):
                pool.wait_ge(s_rt, 19 + n + 1)
                pool.tensor_tensor(y[:, n, :], y[:, n, :], out_b_row, ALU.add).then_inc(s_oa, 1)


def constants():
    q, k = np.arange(P)[:, None], np.arange(2 * P)[None, :]
    lag = q + P - k
    mask = np.where((lag >= 0) & (lag < P), 0.0, MASKED).astype(np.float32)
    row = np.arange(P) % HEAD_DIM
    rot = row < ROT
    freq = np.where(rot, THETA ** (-2.0 * (row % (ROT // 2)) / ROT), 0.0)
    sign = np.where(rot, np.where(row < ROT // 2, -1.0, 1.0), 0.0)
    rope = np.stack([freq, sign, rot * 1.0, 1.0 - rot], 1).astype(np.float32)
    return {"ident": np.eye(P, dtype=np.float32), "ones": np.ones((P, P), np.float32), "mask": mask,
            "rope_c": rope}


def kernel(**inputs):
    import concourse.bacc as bacc
    from concourse.bass_utils import run_bass_kernel_spmd

    nc = bacc.Bacc("TRN2", target_bir_lowering=False, num_devices=1)
    arrays = {}
    for name, a in inputs.items():
        a = np.ascontiguousarray(a)
        arrays[name] = a if name == "c" else a[0]
    arrays.update(constants())
    handles = {name: nc.dram_tensor(name + "_dram", a.shape, mybir.dt.from_np(a.dtype), kind="ExternalInput").ap()
               for name, a in arrays.items()}
    out = nc.dram_tensor("out_dram", (SEQ, D), F32, kind="ExternalOutput").ap()
    build(nc, handles, out)
    r = run_bass_kernel_spmd(nc, [{name + "_dram": a for name, a in arrays.items()}], core_ids=[0])
    return r.results[0]["out_dram"].reshape(1, SEQ, D)
```

```python
from contextlib import ExitStack

import numpy as np

import concourse.bass as bass
import concourse.mybir as mybir
from concourse.alu_op_type import AluOpType as ALU

F32 = mybir.dt.float32
F32R = mybir.dt.float32r
I32 = mybir.dt.int32
ACT = mybir.ActivationFunctionType
AXX = mybir.AxisListType.X

P = 128
D = 1024
SEQ = 1024
KT = D // P
TT = SEQ // P
HALF = 512
D_FF = 2816
FC = D_FF // (2 * P)
HEAD_DIM = 64
N_HEADS = 8
PAIRS = N_HEADS // 2
ATTN_W = 512
CONV_W = 512
KV_W = 128
U0 = ATTN_W + 2 * KV_W
BG0 = U0 + CONV_W
CG0 = BG0 + CONV_W
ROT = 16
THETA = 500000.0
LN_EPS = 1e-5
ALPHA = 2.0 ** 0.25
SCALE = HEAD_DIM ** -0.5
MASKED = -1.0e30
N_MOD = 9
STRIPS = N_MOD * D // HALF
STRIPS_BEFORE = STRIPS - FC
PI = float(np.pi)

UNITS_FFN = 4 * FC
MIX0 = UNITS_FFN
FFN2_0 = MIX0 + 2 + 4 * PAIRS
CHUNK_MIX = FC
CHUNK_FFN2 = FC + PAIRS
PROD_MIX = 2 * FC
PROD_FFN2 = PROD_MIX + PAIRS

COL_C = 0
COL_LN = 8
COL_BADA = 40
COL_CONV = 112
N_COLS = 124

TWO_PI_1 = 6.28125
TWO_PI_2 = float(np.round((2 * np.pi - TWO_PI_1) * 2.0 ** 21) / 2.0 ** 21)
TWO_PI_3 = float(2 * np.pi - TWO_PI_1 - TWO_PI_2)
ROUND_1 = 1.5 * 2.0 ** 23
ROUND_2K = 1.5 * 2.0 ** 34
ROPE_STEPS = 19


def unit(base, c, k):
    return base + 4 * c + k, base // 2 + 2 * c + k // 2, k % 2


def build(nc, t, out):
    with ExitStack() as ctx:
        def sb(name, shape, dt=F32):
            return ctx.enter_context(nc.sbuf_tensor(name, shape, dt))

        def sem(name):
            return ctx.enter_context(nc.semaphore(name))

        h_hi = sb("h_hi", [P, KT, SEQ], F32R)
        h_lo = sb("h_lo", [P, KT, SEQ], F32R)
        act_hi = sb("act_hi", [P, 2, SEQ], F32R)
        act_lo = sb("act_lo", [P, 2, SEQ], F32R)
        wu_hi = sb("wu_hi", [P, 2, D], F32R)
        wu_lo = sb("wu_lo", [P, 2, D], F32R)
        wd_hi = sb("wd_hi", [P, 2, D], F32R)
        wd_lo = sb("wd_lo", [P, 2, D], F32R)
        y = sb("y", [P, TT, D])
        raw_unit = sb("raw_unit", [P, 2, D])
        raw_down = sb("raw_down", [P, 2, D])
        arena = sb("arena", [P, 11, D])
        cos_t, sin_t, sg, prod, gate_row, k_t, v_tok, q_t, q_swap = (arena[:, i, :] for i in range(9))
        strip = arena[:, 7:11, :].rearrange("p a (b n) -> p (a b) n", n=HALF)
        scores = arena[:, 9, :].rearrange("p (s h k) -> p s h k", s=2, h=2)
        probsT = arena[:, 10, :].rearrange("p (s k h q) -> p s k h q", s=2, k=2, h=2)
        strip_acc = [k_t[:, 0:HALF], k_t[:, HALF:]]
        h_tmp = [v_tok[:, 0:HALF], v_tok[:, HALF:], sg[:, 0:HALF], sg[:, HALF:]]
        diag = v_tok
        const_rows = gate_row[0:N_COLS, 0:P]
        v_blk = v_tok.rearrange("p (b n) -> p b n", b=TT)
        rope_w = q_t.rearrange("p (s n) -> p s n", n=SEQ // 16)
        ln_g_row, ln_b_row = arena[:, 9, :], arena[:, 10, :]
        out_g_row, out_b_row = q_t, q_swap
        mask = sb("mask", [P, 2 * P])
        ident = sb("ident", [P, P])
        ones = sb("ones", [P, P])
        rope_c = sb("rope_c", [P, 1])
        cols = sb("cols", [P, N_COLS])
        cond = sb("cond", [P, KT])
        mod = sb("mod", [P, 8 * N_MOD])
        affine = sb("affine", [P, 3, 2, KT])
        gate_c = sb("gate_c", [P, KT])
        sink = sb("sink", [P, 2, PAIRS])
        ln_s = sb("ln_s", [P, 2, 24])
        at_s = sb("at_s", [P, 2, 16])

        ps_unit = [ctx.enter_context(nc.psum_tensor(f"ps_unit{i}", [P, 2, HALF], F32)) for i in range(2)]
        ps_down = [ctx.enter_context(nc.psum_tensor(f"ps_down{i}", [P, 2, HALF], F32)) for i in range(2)]
        ps_mod = ps_down[1][:, 0, 0:4]
        ps_score = ps_down[0]
        ps_probsT = ps_down[1][:, 0, :].rearrange("p (k h q) -> p k h q", k=2, h=2)
        ps_attn = ps_down[1][:, 1, :]

        def flat(p):
            return p[:].rearrange("p a b -> p (a b)")

        s_const = sem("const_loaded")
        s_sink = sem("sink_loaded")
        s_x = [sem(f"x_loaded{i}") for i in range(2)]
        s_colsT = sem("cols_transposed")
        s_cols = sem("cols_copied")
        s_cond = sem("cond_ready")
        s_strip = [sem(f"strip_loaded{i}") for i in range(2)]
        s_acc = sem("strip_products")
        s_modmm = sem("mod_summed")
        s_mod = sem("mod_ready")
        s_aff = sem("affine_ready")
        s_diag = sem("gate_diagonal")
        s_gatemm = sem("gate_spread")
        s_gate = sem("gate_row_ready")
        s_rawu = [sem(f"unit_weights_loaded{i}") for i in range(2)]
        s_whi = sem("unit_weights_hi")
        s_wlo = sem("unit_weights_split")
        s_unit = sem("unit_done")
        s_pfree = [sem(f"unit_psum_read{i}") for i in range(2)]
        s_rawd = [sem(f"down_weights_loaded{i}") for i in range(2)]
        s_dgate = sem("down_weights_gated")
        s_dhi = sem("down_weights_hi")
        s_dlo = sem("down_weights_split")
        s_prod = sem("product_ready")
        s_phi = sem("product_hi")
        s_act = [sem(f"act_ready{i}") for i in range(2)]
        s_down = sem("down_tile_done")
        s_y = sem("y_added")
        s_ln = sem("ln_steps")
        s_var = sem("variance_ready")
        s_std = sem("deviation_ready")
        s_stat = sem("ln_scale_ready")
        s_norm = sem("rows_normalised")
        s_tr = sem("rows_transposed")
        s_ev = sem("h_affine_done")
        s_hhi = sem("h_hi_ready")
        s_rcp = sem("deviation_inverted")
        s_newton = sem("newton_steps")
        s_resd = sem("residual_ready_vector")
        s_rmd = sem("residual_scaled_vector")
        s_h = sem("h_ready")
        s_rows = sem("ln_rows_loaded")
        s_rowsc = sem("ln_rows_scaled")
        s_rm = sem("residual_scaled")
        s_res = sem("residual_ready")
        s_pos = sem("positions_loaded")
        s_rt = sem("rope_table_steps")
        s_sin = sem("sines_ready")
        s_rtab = sem("rope_values_ready")
        s_rbase = sem("rope_tables_filled")
        s_rdram = sem("rope_values_stored")
        s_rload = sem("rope_tables_loaded")
        s_zero = sem("swap_zeroed")
        s_swap = sem("rotary_rows_swapped")
        s_rs = sem("rope_steps")
        s_rope = sem("rope_done")
        s_vT = sem("v_transposed")
        s_v = sem("v_ready")
        s_conv = sem("conv_steps")
        s_sc = sem("scores_ready")
        s_sm = sem("softmax_steps")
        s_msk = sem("scores_masked")
        s_max = sem("maximum_ready")
        s_exp = sem("exponentials_ready")
        s_p = sem("probs_ready")
        s_pT = sem("probs_transposed")
        s_pTc = sem("probsT_copied")
        s_pv = sem("values_summed")
        s_ahi = sem("attention_hi")
        s_alo = sem("attention_split")
        s_ow = sem("out_affine_loaded")
        s_og = sem("out_gained")
        s_ogp = sem("out_gained_gpsimd")
        s_oa = sem("out_rows_ready")
        s_out = sem("out_stored")

        w_gu = [t["ffn1_w_gate_up"], t["ffn2_w_gate_up"]]
        w_dn = [t["ffn1_w_down"], t["ffn2_w_down"]]
        rope_dram = nc.dram_tensor("rope_values", (3, P, SEQ // 16), F32, kind="Internal").ap()
        block = ctx.enter_context(nc.Block())

        def acc_of(n):
            return strip_acc[n % 2 if isinstance(n, int) and n < STRIPS_BEFORE else 1]

        @block.sync
        def _(sp):
            def wait_place(sem_, value):
                if not isinstance(value, int):
                    value = sp.to_reg(value)
                    sp.wait_ge(s_sink, 16)
                sp.wait_ge(sem_, value)

            def load_strip(n):
                for i in range(2):
                    free = None if isinstance(n, int) and n == 0 else sp.snap(8 * n - 4 + 4 * i)
                    src = t["w_ada"][HALF * i:HALF * (i + 1), bass.ds(HALF * n, HALF)]
                    if free is not None:
                        wait_place(s_acc, free)
                    sp.dma_start(strip[:, 4 * i:4 * i + 4, :], src.rearrange("(k p) n -> p k n", p=P)
                                 ).then_inc(s_strip[i], 16)

            def unit_columns(n, c, k):
                if isinstance(n, int) and MIX0 <= n < FFN2_0:
                    j, kind = divmod(n - MIX0 - 3, 4)
                    if n == MIX0:
                        col = ATTN_W
                    elif n == MIX0 + 2:
                        col = ATTN_W + KV_W
                    elif n == MIX0 + 1 or kind == 3:
                        j = 0 if n == MIX0 + 1 else j + 1
                        for h in range(2):
                            col = HEAD_DIM * (j + PAIRS * h)
                            yield (raw_unit[:, k % 2, :].rearrange("p (k h n) -> p h k n", k=KT, h=2)[:, h],
                                   t["w_in"][:, col:col + HEAD_DIM].rearrange("(k p) n -> p k n", p=P))
                        return
                    else:
                        col = (U0, CG0, BG0)[kind] + P * j
                    w = t["w_in"]
                else:
                    w = w_gu[0 if k is not None and c[0] == 0 else 1]
                    col = (0, D_FF, P, D_FF + P)[k] + 2 * P * c[1]
                for i in range(2):
                    yield (raw_unit[:, k % 2, HALF * i:HALF * (i + 1)].rearrange("p (k n) -> p k n", n=P),
                           w[HALF * i:HALF * (i + 1), bass.ds(col, P)].rearrange("(k p) n -> p k n", p=P))

            def load_unit(n, c, k):
                pieces = list(unit_columns(n, c, k))
                if not (isinstance(n, int) and n < 2):
                    wait_place(s_wlo, sp.snap(n - 1))
                for dst, src in pieces:
                    sp.dma_start(dst, src).then_inc(s_rawu[k % 2], 16)

            def load_down(q, i, src0, src1):
                free = None if isinstance(q, int) and q == 0 else sp.snap(2 * q + i - 1)
                srcs = [w[bass.ds(r, 64), :] for w, r in (src0, src1)]
                if free is not None:
                    wait_place(s_dlo, free)
                for m, src in enumerate(srcs):
                    sp.dma_start(raw_down[64 * m:64 * m + 64, i, :], src).then_inc(s_rawd[i], 16)

            def load_down_ffn(f, c):
                q = (0, CHUNK_FFN2)[f] + c
                for i in range(2):
                    r = 2 * P * c + P * i
                    load_down(q, i, (w_dn[f], r), (w_dn[f], r + 64))

            def load_down_mix(j):
                load_down(CHUNK_MIX + j, 0, (t["w_out"], HEAD_DIM * j), (t["w_out"], HEAD_DIM * (PAIRS + j)))
                load_down(CHUNK_MIX + j, 1, (t["w_out"], ATTN_W + P * j), (t["w_out"], ATTN_W + P * j + 64))

            def ffn_body(f, c, strip_n=None):
                base = (0, FFN2_0)[f]
                load_unit(base + 4 * c + 4, (f, c + 1), 0)
                if strip_n is not None:
                    load_strip(strip_n)
                load_unit(base + 4 * c + 5, (f, c + 1), 1)
                load_unit(base + 4 * c + 6, (f, c + 1), 2)
                load_down_ffn(f, c + 1)
                load_unit(base + 4 * c + 7, (f, c + 1), 3)

            for dst, src in ((const_rows[COL_C:COL_LN, :], t["c"].rearrange("a (r n) -> (a r) n", n=P)),
                             (const_rows[8:16, :], t["ln1_g"].rearrange("(r n) -> r n", n=P)),
                             (const_rows[16:24, :], t["ln1_b"].rearrange("(r n) -> r n", n=P)),
                             (const_rows[24:32, :], t["ln2_g"].rearrange("(r n) -> r n", n=P)),
                             (const_rows[32:40, :], t["ln2_b"].rearrange("(r n) -> r n", n=P)),
                             (const_rows[COL_BADA:COL_CONV, :], t["b_ada"].rearrange("(r n) -> r n", n=P)),
                             (const_rows[COL_CONV:N_COLS, :], t["conv_w"].rearrange("a (r n) -> (a r) n", n=P)),
                             (ident[:], t["ident"][:, :]), (ones[:], t["ones"][:, :]), (mask[:], t["mask"][:, :]),
                             (rope_c[:], t["rope_c"][:, :])):
                sp.dma_start(dst, src).then_inc(s_const, 16)
            sp.dma_start(sink[:].rearrange("p h j -> p (h j)"),
                         t["attn_sinks"].partition_broadcast(P)).then_inc(s_sink, 16)
            def load_x(half):
                for n in range(4 * half, 4 * half + 4):
                    sp.dma_start(y[:, n, :], t["x"][P * n:P * n + P, :]).then_inc(s_x[half], 16)

            load_strip(0)
            load_strip(1)
            load_x(0)
            load_strip(2)
            load_strip(3)
            load_unit(0, (0, 0), 0)
            load_x(1)
            load_unit(1, (0, 0), 1)
            load_unit(2, (0, 0), 2)
            load_strip(4)
            load_strip(5)
            load_unit(3, (0, 0), 3)
            load_down_ffn(0, 0)
            load_strip(6)
            ffn_body(0, 0, 7)
            with sp.Fori(1, FC - 1) as c:
                ffn_body(0, c, STRIPS_BEFORE + c)
            load_unit(MIX0, None, 0)
            load_strip(STRIPS - 1)
            load_unit(MIX0 + 1, None, 1)
            sp.wait_ge(s_acc, 8 * STRIPS)
            for f in range(ROT // 2):
                sp.dma_start(rope_w[16 * f:16 * f + 16, 0, :].bitcast(I32),
                             t["positions"].rearrange("(b n) -> b n", b=16)).then_inc(s_pos, 16)
            load_down_mix(0)
            sp.dma_start(ln_g_row, t["ln1_g"].partition_broadcast(P)).then_inc(s_rows, 16)
            sp.dma_start(ln_b_row, t["ln1_b"].partition_broadcast(P)).then_inc(s_rows, 16)
            sp.wait_ge(s_rtab, 1)
            sp.wait_ge(s_sin, 2)
            for i, w in enumerate((3, 2, 4)):
                sp.dma_start(rope_dram[i], rope_w[:, w, :]).then_inc(s_rdram, 16)
            sp.wait_ge(s_rdram, 48)
            sp.wait_ge(s_rbase, 2)
            for h in (0, 64):
                for row, dst, i in ((h, cos_t, 0), (h + 8, cos_t, 0), (h, sin_t, 2), (h + 8, sin_t, 1)):
                    sp.dma_start(dst[row:row + 8, :], rope_dram[i].rearrange("(f b) n -> f (b n)", b=16)
                                 ).then_inc(s_rload, 16)
            load_unit(MIX0 + 2, None, 0)
            load_unit(MIX0 + 3, None, 1)
            for j in range(PAIRS):
                n = MIX0 + 4 * j + 4
                load_unit(n, None, 0)
                load_unit(n + 1, None, 1)
                if j + 1 < PAIRS:
                    load_unit(n + 2, None, 0)
                    load_down_mix(j + 1)
                    load_unit(n + 3, None, 1)
            load_unit(FFN2_0, (1, 0), 0)
            load_unit(FFN2_0 + 1, (1, 0), 1)
            load_down_ffn(1, 0)
            sp.wait_ge(s_pv, TT * PAIRS)
            sp.dma_start(ln_g_row, t["ln2_g"].partition_broadcast(P)).then_inc(s_rows, 16)
            sp.dma_start(ln_b_row, t["ln2_b"].partition_broadcast(P)).then_inc(s_rows, 16)
            sp.dma_start(out_g_row, t["ln3_g"].partition_broadcast(P)).then_inc(s_ow, 32)
            sp.dma_start(out_b_row, t["ln3_b"].partition_broadcast(P)).then_inc(s_ow, 32)
            load_unit(FFN2_0 + 2, (1, 0), 2)
            load_unit(FFN2_0 + 3, (1, 0), 3)
            ffn_body(1, 0)
            with sp.Fori(1, FC - 1) as c:
                ffn_body(1, c)
            for n in range(TT):
                sp.wait_ge(s_oa, n + 1)
                sp.dma_start(out[P * n:P * n + P, :], y[:, n, :]).then_inc(s_out, 16)
            sp.wait_ge(s_out, 16 * TT)

        @block.tensor
        def _(pe):
            def three(ps, st_hi, st_lo, mv_hi, mv_lo, first, last):
                n = len(ps)
                for i in range(n):
                    pe.matmul(ps[i], st_hi, mv_hi[i], start=first, stop=False)
                for i in range(n):
                    pe.matmul(ps[i], st_hi, mv_lo[i], start=False, stop=False)
                for i in range(n):
                    mm = pe.matmul(ps[i], st_lo, mv_hi[i], start=False, stop=last)
                return mm

            def halves(x):
                return [x[:, HALF * i:HALF * (i + 1)] for i in range(2)]

            def unit_kstep(par, k, parts=(0, 1)):
                w = slice(P * k, P * k + P)
                ps = [ps_unit[par][:, i, :] for i in parts]
                hi = [halves(h_hi[:, k, :])[i] for i in parts]
                lo = [halves(h_lo[:, k, :])[i] for i in parts]
                return three(ps, wu_hi[:, par, w], wu_lo[:, par, w], hi, lo, k == 0, k == KT - 1)

            def begin_unit(u):
                n, before, par = u
                pe.wait_ge(s_wlo, n + 1)
                if not (isinstance(before, int) and before == 0):
                    pe.wait_ge(s_pfree[par], before)

            def run_unit(u, beside=()):
                begin_unit(u)
                for k in range(KT):
                    mm = unit_kstep(u[2], k)
                    if k == KT - 1:
                        mm.then_inc(s_unit, 1)
                    if k < len(beside) and beside[k]:
                        beside[k]()

            def down_part(q, n, i, mods=None):
                if n == 0:
                    pe.wait_ge(s_dlo, 2 * q + i + 1)
                    pe.wait_ge(s_act[i], q + 1)
                if i == 0 and not (isinstance(q, int) and q == 0 and n < 2):
                    pe.wait_ge(s_y, 8 * q + n - 1)
                if i == 0 and n == 1 and mods is not None:
                    pe.wait_ge(s_mod, mods)
                ps = [ps_down[n % 2][:, m, :] for m in range(2)]
                tok = slice(P * n, P * n + P)
                return three(ps, act_hi[:, i, tok], act_lo[:, i, tok], halves(wd_hi[:, i, :]),
                             halves(wd_lo[:, i, :]), i == 0, i == 1)

            def down_all(q, tiles=range(TT), mods=None):
                tiles = list(tiles)
                if 0 in tiles:
                    for i in range(2):
                        for n in range(2):
                            mm = down_part(q, n, i, mods)
                            if i == 1:
                                mm.then_inc(s_down, 1)
                    tiles = tiles[2:]
                for n in tiles:
                    down_part(q, n, 0)
                    down_part(q, n, 1).then_inc(s_down, 1)

            def transpose_rows(stage, half, d):
                if stage == 0:
                    pe.wait_ge(s_x[half], 64)
                else:
                    pe.wait_ge(s_norm, 8 * (stage - 1) + 4 * half + 4)
                n = 16 * stage + 8 * half + d
                if half == 0 and d == 0 and stage > 0:
                    pe.wait_ge(s_pfree[1], (0, MIX0 // 2, FFN2_0 // 2)[stage])
                if n >= 2:
                    pe.wait_ge(s_ev, n - 1)
                for i in range(4):
                    mm = pe.transpose(ps_unit[1][:, n % 2, P * i:P * i + P],
                                      y[:, 4 * half + i, P * d:P * d + P], ident[:])
                mm.then_inc(s_tr, 1)

            def first_unit(stage, base):
                begin_unit(unit(base, 0, 0))
                steps = [(half, d) for half in range(2) for d in range(KT)]
                for i in range(2, len(steps) + 3):
                    if i < len(steps):
                        transpose_rows(stage, *steps[i])
                    if i >= 3:
                        half, d = steps[i - 3]
                        pe.wait_ge(s_h, 16 * stage + i - 2)
                        mm = unit_kstep(0, d, (half,))
                mm.then_inc(s_unit, 1)
                pe.wait_ge(s_ev, 16 * (stage + 1))

            def down_and_turn(q, stage, mods=None):
                down_all(q, range(TT - 1), mods)
                transpose_rows(stage, 0, 0)
                transpose_rows(stage, 0, 1)
                down_all(q, (TT - 1,))

            def sum_strip(n, q=0):
                pe.wait_ge(s_acc, 8 * n + 8)
                if not isinstance(n, int) or n > 0:
                    pe.wait_ge(s_mod, n)
                if not isinstance(q, int) or q > 0:
                    pe.wait_ge(s_y, 8 * q)
                for i in range(4):
                    mm = pe.matmul(ps_mod[:, i:i + 1], acc_of(n)[:, P * i:P * i + P], ones[:, 0:1],
                                   start=True, stop=True)
                mm.then_inc(s_modmm, 1)

            def spread_gate(stage, q):
                pe.wait_ge(s_diag, stage + 1)
                if q > 0:
                    pe.wait_ge(s_y, 8 * q)
                for d in range(KT):
                    mm = pe.matmul(ps_down[0][:, d // 4, P * (d % 4):P * (d % 4) + P], ones[:],
                                   diag[:, P * d:P * d + P], start=True, stop=True)
                mm.then_inc(s_gatemm, 1)

            def ffn_body(f, c, strip_n=None, after_up=None, after_gate=None, last=False):
                base, q0 = ((0, 0), (FFN2_0, CHUNK_FFN2))[f]
                run_unit(unit(base, c, 1))
                if after_up:
                    after_up()
                run_unit(unit(base, c, 2))
                if after_gate:
                    after_gate()
                run_unit(unit(base, c, 3))
                if strip_n is not None and last:
                    sum_strip(strip_n, q0 + c)
                if last:
                    return
                run_unit(unit(base, c, 4))
                if strip_n is not None:
                    sum_strip(strip_n, q0 + c)
                down_all(q0 + c, mods=None if strip_n is None else strip_n + 1)

            pe.wait_ge(s_const, 16 * 11)
            pe.transpose(ps_unit[0][:, 0, 0:N_COLS], const_rows, ident[0:N_COLS, 0:N_COLS]
                         ).then_inc(s_colsT, 1)
            transpose_rows(0, 0, 0)
            transpose_rows(0, 0, 1)
            for n in range(4):
                sum_strip(n)
            pe.wait_ge(s_cols, 1)
            first_unit(0, 0)

            def g1_columns():
                sum_strip(4)
                sum_strip(5)

            def g1_row():
                spread_gate(0, 0)
                sum_strip(6)

            ffn_body(0, 0, 7, g1_columns, g1_row)
            with pe.Fori(1, FC - 1) as c:
                ffn_body(0, c, STRIPS_BEFORE + c)
            ffn_body(0, FC - 1, STRIPS - 1, last=True)
            down_and_turn(FC - 1, 1, STRIPS)

            first_unit(1, MIX0)
            run_unit(unit(MIX0, 0, 1))
            spread_gate(1, FC)
            run_unit(unit(MIX0, 0, 2))
            pe.wait_ge(s_pfree[0], MIX0 // 2 + 2)
            pe.wait_ge(s_gate, 2)
            for b in range(TT):
                mm = pe.transpose(ps_down[0][:, b // 4, P * (b % 4):P * (b % 4) + P],
                                  sg[:, P * b:P * b + P], ident[:])
            mm.then_inc(s_vT, 1)

            def score(j, b):
                n = TT * j + b
                if b == 0:
                    pe.wait_ge(s_rope, 2 + j)
                    pe.wait_ge(s_v, 1)
                    pe.wait_ge(s_y, 8 * (CHUNK_MIX + j))
                if n >= 1:
                    pe.wait_ge(s_msk, n)
                k0 = P * (b - 1) if b else 0
                for h in range(2):
                    r = slice(64 * h, 64 * h + 64)
                    o0 = 256 * (b % 2)
                    mm = pe.matmul(ps_score[:, h, o0 + (0 if b else P):o0 + 256], q_t[r, P * b:P * b + P],
                                   k_t[r, k0:P * b + P], start=True, stop=True)
                mm.then_inc(s_sc, 1)

            def turn_probs(j, b):
                n = TT * j + b
                pe.wait_ge(s_p, n + 1)
                if n >= 1:
                    pe.wait_ge(s_pTc, n)
                for k in range(0 if b else 1, 2):
                    for h in range(2):
                        mm = pe.transpose(ps_probsT[:, k, h, :], scores[:, b % 2, h, P * k:P * k + P],
                                          ident[:])
                mm.then_inc(s_pT, 1)

            def values(j, b):
                n = TT * j + b
                pe.wait_ge(s_pTc, n + 1)
                if b % 4 == 0 and n >= 4:
                    pe.wait_ge(s_alo, n // 4)
                for h in range(2):
                    for k in range(0 if b else 1, 2):
                        mm = pe.matmul(ps_attn[64 * h:64 * h + 64, P * (b % 4):P * (b % 4) + P],
                                       v_blk[:, b - 1 + k, 64 * h:64 * h + 64], probsT[:, b % 2, k, h, :],
                                       start=k == (0 if b else 1), stop=k == 1)
                mm.then_inc(s_pv, 1)

            for j in range(PAIRS):
                steps = [None] * 32
                for b in range(TT):
                    steps[3 * b] = lambda b=b: score(j, b)
                    steps[3 * b + 5] = lambda b=b: turn_probs(j, b)
                    steps[3 * b + 7] = lambda b=b: values(j, b)
                run_unit(unit(MIX0, j, 3), steps[0:8])
                run_unit(unit(MIX0, j, 4), steps[8:16])
                run_unit(unit(MIX0, j, 5), steps[16:24])
                if j + 1 < PAIRS:
                    run_unit(unit(MIX0, j, 6), steps[24:32])
                    down_all(CHUNK_MIX + j)
                else:
                    for s in steps[24:32]:
                        if s:
                            s()
            down_and_turn(CHUNK_MIX + PAIRS - 1, 2)

            first_unit(2, FFN2_0)
            ffn_body(1, 0, after_gate=lambda: spread_gate(2, CHUNK_FFN2))
            with pe.Fori(1, FC - 1) as c:
                ffn_body(1, c)
            ffn_body(1, FC - 1, last=True)
            down_all(CHUNK_FFN2 + FC - 1)

        @block.scalar
        def _(act):
            def split_unit(u):
                n, before, par = u
                act.wait_ge(s_rawu[par], 32 * before + 32)
                if not (isinstance(n, int) and n < 2):
                    act.wait_ge(s_unit, n - 1)
                act.activation(wu_hi[:, par, :], raw_unit[:, par, :], ACT.Copy).then_inc(s_whi, 1)

            def split_down(q):
                for i in range(2):
                    act.wait_ge(s_dgate, 2 * q + i + 1)
                    if not (isinstance(q, int) and q == 0):
                        act.wait_ge(s_down, 8 * q)
                    act.activation(wd_hi[:, i, :], raw_down[:, i, :], ACT.Copy).then_inc(s_dhi, 1)

            def silu_gate(u):
                n, before, par = u
                act.wait_ge(s_unit, n + 1)
                if not (isinstance(before, int) and before == 0):
                    act.wait_ge(s_pfree[1], before)
                act.activation(sg, flat(ps_unit[par]), ACT.Silu).then_inc(s_pfree[par], 1)

            def h_taken(stage):
                act.wait_ge(s_h, 16 * (stage + 1))

            def product_hi(m, i, q):
                act.wait_ge(s_prod, m + 1)
                if not (isinstance(q, int) and q == 0):
                    act.wait_ge(s_down, 8 * q)
                act.activation(act_hi[:, i, :], prod, ACT.Copy).then_inc(s_phi, 1)

            def h_out(stage, half, d):
                n = 16 * stage + 8 * half + d
                act.wait_ge(s_tr, n + 1)
                act.wait_ge(s_aff, stage + 1)
                if n >= 4:
                    act.wait_ge(s_h, n - 3)
                act.activation(h_tmp[n % 4], ps_unit[1][:, n % 2, :], ACT.Identity,
                               bias=affine[:, stage, 1, d:d + 1], scale=affine[:, stage, 0, d:d + 1]
                               ).then_inc(s_ev, 1)

            def deviation(ln, n):
                m = TT * ln + n
                act.wait_ge(s_var, m + 1)
                act.activation(ln_s[:, n % 2, 15:16], ln_s[:, n % 2, 14:15], ACT.Sqrt).then_inc(s_std, 1)

            def normalise(ln, n):
                m = TT * ln + n
                act.wait_ge(s_stat, m + 1)
                act.activation(y[:, n, :], y[:, n, :], ACT.Identity, bias=ln_s[:, n % 2, 21:22],
                               scale=ln_s[:, n % 2, 20:21]).then_inc(s_norm, 1)

            def ln_turn(stage):
                for n in range(TT):
                    deviation(stage - 1, n)
                    normalise(stage - 1, n)
                    for d in {5: (0, 1), 6: (2, 3, 4), 7: (5, 6, 7)}.get(n, ()):
                        h_out(stage, 0, d)
                for d in range(KT):
                    h_out(stage, 1, d)

            def ffn_body(f, c, last=False, gate=None):
                base, q0, m0 = ((0, 0, 0), (FFN2_0, CHUNK_FFN2, PROD_FFN2))[f]
                split_unit(unit(base, c, 2))
                split_unit(unit(base, c, 3))
                product_hi(m0 + 2 * c, 0, q0 + c)
                silu_gate(unit(base, c, 2))
                if gate is not None:
                    gate_out(gate)
                if not (last and f):
                    split_unit(unit(base, c, 4))
                split_down(q0 + c)
                if not (last and f):
                    split_unit(unit(base, c, 5))
                product_hi(m0 + 2 * c + 1, 1, q0 + c)
                if not last:
                    silu_gate(unit(base, c, 4))

            def gate_out(stage):
                act.wait_ge(s_gatemm, stage + 1)
                q = (0, CHUNK_MIX, CHUNK_FFN2)[stage]
                if q:
                    act.wait_ge(s_dgate, 2 * q)
                act.activation(gate_row, flat(ps_down[0]), ACT.Copy).then_inc(s_gate, 1)

            act.wait_ge(s_cols, 1)
            act.activation(cond[:], cols[:, COL_C:COL_C + KT], ACT.Silu).then_inc(s_cond, 1)
            split_unit(unit(0, 0, 0))
            split_unit(unit(0, 0, 1))
            for half in range(2):
                for d in range(KT):
                    h_out(0, half, d)
            h_taken(0)
            silu_gate(unit(0, 0, 0))
            ffn_body(0, 0, gate=0)
            with act.Fori(1, FC - 1) as c:
                ffn_body(0, c)
            ffn_body(0, FC - 1, last=True)
            act.wait_ge(s_rt, ROPE_STEPS)
            act.activation(rope_w[:, 2, :], rope_w[:, 2, :], ACT.Sin).then_inc(s_sin, 1)
            act.activation(rope_w[:, 3, :], rope_w[:, 3, :], ACT.Sin).then_inc(s_sin, 1)
            ln_turn(1)

            def copy_out(dst, u):
                n, before, par = u
                act.wait_ge(s_unit, n + 1)
                act.activation(dst, flat(ps_unit[par]), ACT.Copy).then_inc(s_pfree[par], 1)

            def swap_rotary(src, r):
                act.wait_ge(s_zero, 1)
                if r > 0:
                    act.wait_ge(s_rope, r)
                for b in (0, 64):
                    act.dma_start(q_swap[b:b + 8, :], src[b + 8:b + 16, :]).then_inc(s_swap, 16)
                    act.dma_start(q_swap[b + 8:b + 16, :], src[b:b + 8, :]).then_inc(s_swap, 16)

            split_unit(unit(MIX0, 0, 2))
            copy_out(k_t, unit(MIX0, 0, 0))
            act.wait_ge(s_pfree[0], MIX0 // 2 + 1)
            swap_rotary(k_t, 0)
            split_unit(unit(MIX0, 0, 3))
            act.wait_ge(s_rload, 128)
            copy_out(q_t, unit(MIX0, 0, 1))
            act.wait_ge(s_pfree[1], MIX0 // 2 + 1)
            swap_rotary(q_t, 1)
            gate_out(1)
            h_taken(1)
            copy_out(sg, unit(MIX0, 0, 2))
            act.wait_ge(s_vT, 1)
            act.activation(v_tok, flat(ps_down[0]), ACT.Copy).then_inc(s_v, 1)
            split_down(CHUNK_MIX)

            def exps(j, b):
                n = TT * j + b
                k0 = 0 if b else P
                act.wait_ge(s_max, n + 1)
                for h in range(2):
                    act.activation(scores[:, b % 2, h, k0:], scores[:, b % 2, h, k0:], ACT.Exp,
                                   bias=at_s[:, b % 2, 2 + h:3 + h],
                                   accum_out=at_s[:, b % 2, 6 + h:7 + h])
                act.activation(at_s[:, b % 2, 8:10], at_s[:, b % 2, 4:6], ACT.Exp).then_inc(s_exp, 1)

            def probsT_out(j, b):
                n = TT * j + b
                act.wait_ge(s_pT, n + 1)
                if n >= 2:
                    act.wait_ge(s_pv, n - 1)
                k0 = 0 if b else 1
                act.activation(probsT[:, b % 2, k0:], ps_probsT[:, k0:], ACT.Copy).then_inc(s_pTc, 1)

            def attn_hi(j, g):
                act.wait_ge(s_pv, TT * j + 4 * g + 4)
                act.wait_ge(s_down, 8 * (CHUNK_MIX + j))
                act.activation(act_hi[:, 0, HALF * g:HALF * (g + 1)], ps_attn, ACT.Copy).then_inc(s_ahi, 1)

            for j in range(PAIRS):
                last = j + 1 == PAIRS
                exps(j, 0)
                exps(j, 1)
                probsT_out(j, 0)
                split_unit(unit(MIX0, j, 4))
                exps(j, 2)
                probsT_out(j, 1)
                act.wait_ge(s_prod, PROD_MIX + j)
                copy_out(sg, unit(MIX0, j, 3))
                split_unit(unit(MIX0, j, 5))
                exps(j, 3)
                probsT_out(j, 2)
                exps(j, 4)
                probsT_out(j, 3)
                exps(j, 5)
                attn_hi(j, 0)
                probsT_out(j, 4)
                split_unit(unit(MIX0, j, 6) if not last else unit(FFN2_0, 0, 0))
                exps(j, 6)
                probsT_out(j, 5)
                exps(j, 7)
                probsT_out(j, 6)
                product_hi(PROD_MIX + j, 1, CHUNK_MIX + j)
                probsT_out(j, 7)
                split_unit(unit(MIX0, j, 7) if not last else unit(FFN2_0, 0, 1))
                attn_hi(j, 1)
                if not last:
                    copy_out(q_t, unit(MIX0, j, 6))
                    act.wait_ge(s_pfree[0], MIX0 // 2 + 4 + 2 * j)
                    swap_rotary(q_t, 2 + j)
                    split_down(CHUNK_MIX + j + 1)
            ln_turn(2)

            h_taken(2)
            silu_gate(unit(FFN2_0, 0, 0))
            ffn_body(1, 0, gate=2)
            with act.Fori(1, FC - 1) as c:
                ffn_body(1, c)
            ffn_body(1, FC - 1, last=True)
            for n in range(TT):
                deviation(2, n)
                normalise(2, n)

        @block.vector
        def _(dve):
            def split_unit(u):
                n, before, par = u
                dve.wait_ge(s_whi, n + 1)
                dve.tensor_tensor(wu_lo[:, par, :], raw_unit[:, par, :], wu_hi[:, par, :].bitcast(F32),
                                  ALU.subtract).then_inc(s_wlo, 1)

            def split_down(q):
                for i in range(2):
                    dve.wait_ge(s_dhi, 2 * q + i + 1)
                    dve.tensor_tensor(wd_lo[:, i, :], raw_down[:, i, :], wd_hi[:, i, :].bitcast(F32),
                                      ALU.subtract).then_inc(s_dlo, 1)

            def glu(u, m, i, q):
                n, before, par = u
                dve.wait_ge(s_unit, n + 1)
                dve.wait_ge(s_pfree[0], before + 1)
                if not (isinstance(q, int) and q == 0 and i == 0):
                    dve.wait_ge(s_act[1 - i], q + i)
                dve.tensor_tensor(prod, sg, flat(ps_unit[par]), ALU.mult).then_inc(s_pfree[par], 1)

            def product_lo(m, i):
                dve.wait_ge(s_phi, m + 1)
                dve.tensor_tensor(act_lo[:, i, :], prod, act_hi[:, i, :].bitcast(F32),
                                  ALU.subtract).then_inc(s_act[i], 1)

            def strip_products(n):
                for k in range(KT):
                    if k % 4 == 0:
                        dve.wait_ge(s_strip[k // 4], 16 * n + 16)
                    acc = acc_of(n)
                    if k == 0:
                        early = isinstance(n, int) and n <= STRIPS_BEFORE
                        if not (early and n < 2):
                            dve.wait_ge(s_modmm, n - 1 if early else n)
                        dve.tensor_scalar(acc, strip[:, 0, :], cond[:, 0:1], None, ALU.mult
                                          ).then_inc(s_acc, 1)
                        continue
                    dve.wait_ge(s_acc, 8 * n + k)
                    dve.scalar_tensor_tensor(acc, strip[:, k, :], cond[:, k:k + 1], acc,
                                             ALU.mult, ALU.add).then_inc(s_acc, 1)

            def mod_out(n):
                dve.wait_ge(s_modmm, n + 1)
                dve.tensor_tensor(mod[:, bass.ds(4 * n, 4)], ps_mod, cols[:, bass.ds(COL_BADA + 4 * n, 4)],
                                  ALU.add).then_inc(s_mod, 1)

            def affine_cols(stage):
                sh, sc = mod[:, 24 * stage:24 * stage + 8], mod[:, 24 * stage + 8:24 * stage + 16]
                a, b = affine[:, stage, 0, :], affine[:, stage, 1, :]
                if stage == 0:
                    dve.tensor_scalar(a, sc, 1.0, None, ALU.add).then_inc(s_ln, 1)
                    dve.tensor_scalar(b, sh, 0.0, None, ALU.add).then_inc(s_ln, 1)
                    dve.wait_ge(s_ln, steps(2))
                    dve.nop().then_inc(s_aff, 1)
                    return
                g = cols[:, COL_LN + 16 * (stage - 1):COL_LN + 16 * (stage - 1) + 8]
                lb = cols[:, COL_LN + 16 * (stage - 1) + 8:COL_LN + 16 * stage]
                dve.scalar_tensor_tensor(a, sc, 1.0, g, ALU.add, ALU.mult).then_inc(s_ln, 1)
                dve.scalar_tensor_tensor(b, sc, 1.0, lb, ALU.add, ALU.mult).then_inc(s_ln, 1)
                dve.wait_ge(s_ln, steps(2))
                dve.tensor_tensor(b, b, sh, ALU.add).then_inc(s_aff, 1)

            ln_count = [0]

            def steps(n):
                ln_count[0] += n
                return ln_count[0]

            def gate_diagonal(stage):
                g = mod[:, 24 * stage + 16:24 * stage + 24]
                factor = (0.5, 1.0, 0.5)[stage]
                dve.tensor_scalar(gate_c[:], g, 1.0, factor, ALU.add, ALU.mult).then_inc(s_ln, 1)
                dve.wait_ge(s_ln, steps(1))
                dve.wait_ge(s_h, 16 * (stage + 1))
                for d in range(KT):
                    ins = dve.tensor_scalar(diag[:, P * d:P * d + P], ident[:], gate_c[:, d:d + 1], None,
                                            ALU.mult)
                ins.then_inc(s_diag, 1)

            def h_split(stage, half, d):
                n = 16 * stage + 8 * half + d
                at = slice(HALF * half, HALF * half + HALF)
                dve.wait_ge(s_ev, n + 1)
                dve.tensor_copy(h_hi[:, d, at], h_tmp[n % 4]).then_inc(s_hhi, 1)
                dve.wait_ge(s_hhi, n + 1)
                dve.tensor_tensor(h_lo[:, d, at], h_tmp[n % 4], h_hi[:, d, at].bitcast(F32),
                                  ALU.subtract).then_inc(s_h, 1)

            def add_y(q, n, stage=None):
                dve.wait_ge(s_down, 8 * q + n + 1)
                if stage is not None:
                    await_residual(stage, n)
                elif not (isinstance(q, int) and q == 0):
                    dve.wait_ge(s_y, 8 * q + n - 7)
                dve.tensor_tensor(y[:, n, :], y[:, n, :], flat(ps_down[n % 2]), ALU.add).then_inc(s_y, 1)

            def residual(stage, n):
                dve.wait_ge(s_tr, 16 * stage + 8 * (n // 4) + 8)
                if stage == 0:
                    dve.tensor_scalar(y[:, n, :], y[:, n, :], ALPHA, None, ALU.mult).then_inc(s_resd, 1)
                    return
                dve.tensor_tensor(y[:, n, :], y[:, n, :], ln_g_row, ALU.mult).then_inc(s_rmd, 1)
                dve.wait_ge(s_rmd, 4 * (stage - 1) + n // 2 + 1)
                dve.tensor_tensor(y[:, n, :], y[:, n, :], ln_b_row, ALU.add).then_inc(s_resd, 1)

            def await_residual(stage, n):
                if stage == 0:
                    dve.wait_ge(s_resd, n + 1)
                elif n % 2:
                    dve.wait_ge(s_resd, TT + 4 * (stage - 1) + n // 2 + 1)
                else:
                    dve.wait_ge(s_res, 4 * (stage - 1) + n // 2 + 1)

            def scale_rows(stage):
                dve.wait_ge(s_rows, 32 * stage)
                for row in (ln_g_row, ln_b_row):
                    dve.tensor_scalar(row, row, ALPHA, None, ALU.mult).then_inc(s_rowsc, 1)
                dve.wait_ge(s_rowsc, 2 * stage)

            def invert(ln, n):
                dve.wait_ge(s_std, TT * ln + n + 1)
                dve.reciprocal(ln_s[:, n % 2, 16:17], ln_s[:, n % 2, 15:16]).then_inc(s_rcp, 1)

            def statistics(ln, q, n):
                s = ln_s[:, n % 2, :]
                m = TT * ln + n
                add_y(q, n)
                if n > 0:
                    invert(ln, n - 1)
                if m >= 2:
                    dve.wait_ge(s_norm, m - 1)
                dve.wait_ge(s_y, 8 * q + n + 1)
                for i in range(2):
                    dve.bn_stats(s[:, 6 * i:6 * i + 6], y[:, n, HALF * i:HALF * i + HALF]).then_inc(s_ln, 1)
                dve.wait_ge(s_ln, steps(2))
                dve.bn_aggr(s[:, 12:14], s[:, 0:12]).then_inc(s_ln, 1)
                dve.wait_ge(s_ln, steps(1))
                dve.tensor_scalar(s[:, 14:15], s[:, 13:14], LN_EPS, None, ALU.add).then_inc(s_var, 1)

            def ln_turn(stage, q):
                ln = stage - 1
                for n in range(TT - 1):
                    statistics(ln, q, n)
                h_split(stage, 0, 0)
                h_split(stage, 0, 1)
                statistics(ln, q, TT - 1)
                h_split(stage, 0, 2)
                invert(ln, TT - 1)
                for d in range(3, KT):
                    h_split(stage, 0, d)
                for d in range(KT):
                    h_split(stage, 1, d)

            def ffn_body(f, c, strip_n=None, first=False, last=False, after_up=None, between=None):
                base, q0, m0 = ((0, 0, 0), (FFN2_0, CHUNK_FFN2, PROD_FFN2))[f]
                split_unit(unit(base, c, 2))
                if after_up:
                    after_up()
                glu(unit(base, c, 1), m0 + 2 * c, 0, q0 + c)
                dve.wait_ge(s_pfree[1], base // 2 + 2 * c + 1)
                dve.nop().then_inc(s_prod, 1)
                split_unit(unit(base, c, 3))
                product_lo(m0 + 2 * c, 0)
                if between:
                    between()
                if strip_n is not None:
                    strip_products(strip_n)
                if last and not f:
                    rope_angles()
                if not (last and f):
                    split_unit(unit(base, c, 4))
                split_down(q0 + c)
                glu(unit(base, c, 3), m0 + 2 * c + 1, 1, q0 + c)
                dve.wait_ge(s_pfree[1], base // 2 + 2 * c + 2)
                dve.nop().then_inc(s_prod, 1)
                if not (last and f):
                    split_unit(unit(base, c, 5))
                product_lo(m0 + 2 * c + 1, 1)
                if strip_n is not None:
                    mod_out(strip_n)
                if not last:
                    for n in range(TT):
                        add_y(q0 + c, n, 2 * f if first else None)

            dve.wait_ge(s_colsT, 1)
            dve.tensor_copy(cols[:], ps_unit[0][:, 0, 0:N_COLS]).then_inc(s_cols, 1)
            dve.wait_ge(s_cond, 1)
            strip_products(0)
            for n in range(1, 4):
                mod_out(n - 1)
                strip_products(n)
            mod_out(3)
            dve.wait_ge(s_mod, 4)
            affine_cols(0)
            split_unit(unit(0, 0, 0))
            for d in range(KT):
                h_split(0, 0, d)
            split_unit(unit(0, 0, 1))
            for d in range(KT):
                h_split(0, 1, d)
            for n in range(TT):
                residual(0, n)

            def g1_columns():
                for n in (4, 5):
                    strip_products(n)
                for n in (4, 5):
                    mod_out(n)
                dve.wait_ge(s_mod, 6)
                gate_diagonal(0)

            def strip_6():
                strip_products(6)
                mod_out(6)

            def rope_angles():
                done = [0]
                pos, tmp, ang, turns = (rope_w[:, i, :] for i in (0, 1, 3, 2))

                def step(ins):
                    ins.then_inc(s_rt, 1)
                    done[0] += 1
                    dve.wait_ge(s_rt, done[0])
                dve.wait_ge(s_pos, 16 * (ROT // 2))
                step(dve.tensor_copy(tmp, pos.bitcast(I32)))
                step(dve.tensor_scalar(ang, tmp, rope_c[:, 0:1], None, ALU.mult))
                step(dve.tensor_scalar(turns, ang, 1.0 / (2 * PI), None, ALU.mult))
                step(dve.tensor_scalar(turns, turns, ROUND_1, None, ALU.add))
                step(dve.tensor_scalar(turns, turns, -ROUND_1, None, ALU.add))
                step(dve.tensor_scalar(tmp, turns, ROUND_2K, None, ALU.add))
                step(dve.tensor_scalar(tmp, tmp, -ROUND_2K, None, ALU.add))
                step(dve.tensor_tensor(turns, turns, tmp, ALU.subtract))
                for part in (TWO_PI_1, TWO_PI_2, TWO_PI_3):
                    for n in (tmp, turns):
                        step(dve.scalar_tensor_tensor(ang, n, -part, ang, ALU.mult, ALU.add))
                step(dve.tensor_scalar(turns, ang, PI, -PI, ALU.min, ALU.max))
                step(dve.tensor_scalar(ang, ang, PI / 2, None, ALU.add))
                step(dve.tensor_scalar(tmp, ang, PI, -2 * PI, ALU.is_gt, ALU.mult))
                step(dve.tensor_tensor(ang, ang, tmp, ALU.add))
                step(dve.tensor_scalar(ang, ang, PI, -PI, ALU.min, ALU.max))
                assert done[0] == ROPE_STEPS

            ffn_body(0, 0, 7, first=True, after_up=g1_columns, between=strip_6)
            with dve.Fori(1, FC - 1) as c:
                ffn_body(0, c, STRIPS_BEFORE + c)
            ffn_body(0, FC - 1, STRIPS - 1, last=True)
            dve.wait_ge(s_mod, STRIPS)
            affine_cols(1)
            affine_cols(2)
            dve.wait_ge(s_sin, 1)
            dve.tensor_scalar(rope_w[:, 4, :], rope_w[:, 2, :], -1.0, None, ALU.mult).then_inc(s_rtab, 1)
            ln_turn(1, FC - 1)

            gate_diagonal(1)
            split_unit(unit(MIX0, 0, 2))
            scale_rows(1)
            residual(1, 1)

            def rope(dst, r):
                dve.wait_ge(s_swap, 64 * (r + 1))
                dve.tensor_tensor(q_swap, q_swap, sin_t, ALU.mult).then_inc(s_rs, 1)
                dve.tensor_tensor(dst, dst, cos_t, ALU.mult).then_inc(s_rs, 1)
                dve.wait_ge(s_rs, 2 * (r + 1))
                dve.tensor_tensor(dst, dst, q_swap, ALU.add).then_inc(s_rope, 1)

            dve.wait_ge(s_rload, 128)
            rope(k_t, 0)
            residual(1, 3)
            split_unit(unit(MIX0, 0, 3))
            residual(1, 5)
            rope(q_t, 1)
            residual(1, 7)
            split_down(CHUNK_MIX)
            sm = [0]

            def sm_step():
                sm[0] += 1
                return sm[0]

            def softmax_max(j, b):
                n = TT * j + b
                k0 = 0 if b else P
                s = at_s[:, b % 2, :]
                dve.wait_ge(s_sc, n + 1)
                if n >= 2:
                    dve.wait_ge(s_pT, n - 1)
                sc = scores[:, b % 2, :, k0:]
                ps = ps_score[:, :, 256 * (b % 2) + k0:256 * (b % 2) + 256]
                mk = mask[:, k0:].unsqueeze(1).to_broadcast([P, 2, 2 * P - k0])
                dve.scalar_tensor_tensor(sc, ps, SCALE, mk, ALU.mult, ALU.add).then_inc(s_msk, 1)
                dve.wait_ge(s_msk, n + 1)
                dve.tensor_reduce(s[:, 0:2], sc, AXX, ALU.max).then_inc(s_sm, 1)
                dve.wait_ge(s_sm, sm_step())
                dve.tensor_tensor(s[:, 0:2], s[:, 0:2], sink[:, :, j], ALU.max).then_inc(s_sm, 1)
                dve.wait_ge(s_sm, sm_step())
                dve.tensor_scalar(s[:, 2:4], s[:, 0:2], -1.0, None, ALU.mult).then_inc(s_sm, 1)
                dve.wait_ge(s_sm, sm_step())
                dve.tensor_tensor(s[:, 4:6], sink[:, :, j], s[:, 2:4], ALU.add).then_inc(s_max, 1)

            def softmax_norm(j, b):
                n = TT * j + b
                k0 = 0 if b else P
                s = at_s[:, b % 2, :]
                dve.wait_ge(s_exp, n + 1)
                dve.tensor_tensor(s[:, 10:12], s[:, 6:8], s[:, 8:10], ALU.add).then_inc(s_sm, 1)
                dve.wait_ge(s_sm, sm_step())
                dve.reciprocal(s[:, 12:14], s[:, 10:12]).then_inc(s_sm, 1)
                dve.wait_ge(s_sm, sm_step())
                sc = scores[:, b % 2, :, k0:]
                dve.tensor_tensor(sc, sc, s[:, 12:14].unsqueeze(2).to_broadcast([P, 2, 2 * P - k0]),
                                  ALU.mult).then_inc(s_p, 1)

            def attn_lo(j, g):
                dve.wait_ge(s_ahi, 2 * j + g + 1)
                at = slice(HALF * g, HALF * g + HALF)
                dve.tensor_tensor(act_lo[:, 0, at], ps_attn, act_hi[:, 0, at].bitcast(F32), ALU.subtract
                                  ).then_inc(s_alo, 1)
                if g == 1:
                    dve.wait_ge(s_alo, 2 * j + 2)
                    dve.nop().then_inc(s_act[0], 1)

            def conv(j):
                w = [cols[:, COL_CONV + 4 * tap + j:COL_CONV + 4 * tap + j + 1] for tap in range(3)]
                dve.wait_ge(s_unit, MIX0 + 4 * j + 5)
                dve.wait_ge(s_pfree[1], MIX0 // 2 + 2 * j + 2)
                dve.tensor_tensor(sg, sg, flat(ps_unit[0]), ALU.mult).then_inc(s_pfree[0], 1)
                yield
                dve.wait_ge(s_pfree[0], MIX0 // 2 + 2 * j + 3)
                dve.wait_ge(s_act[1], CHUNK_MIX + j)
                dve.tensor_scalar(prod, sg, w[2], None, ALU.mult).then_inc(s_conv, 1)
                for tap in (1, 0):
                    lag = 2 - tap
                    dve.wait_ge(s_conv, 3 * j + lag)
                    dve.scalar_tensor_tensor(prod[:, lag:], sg[:, 0:SEQ - lag], w[tap], prod[:, lag:],
                                             ALU.mult, ALU.add).then_inc(s_conv, 1)
                    yield

            def conv_gate(j):
                dve.wait_ge(s_unit, MIX0 + 4 * j + 6)
                dve.wait_ge(s_conv, 3 * j + 3)
                dve.tensor_tensor(prod, prod, flat(ps_unit[1]), ALU.mult).then_inc(s_pfree[1], 1)
                dve.wait_ge(s_pfree[1], MIX0 // 2 + 2 * j + 3)
                dve.nop().then_inc(s_prod, 1)

            for j in range(PAIRS):
                last = j + 1 == PAIRS
                softmax_max(j, 0)
                softmax_max(j, 1)
                softmax_norm(j, 0)
                split_unit(unit(MIX0, j, 4))
                softmax_max(j, 2)
                softmax_norm(j, 1)
                split_unit(unit(MIX0, j, 5))
                softmax_max(j, 3)
                softmax_norm(j, 2)
                softmax_max(j, 4)
                softmax_norm(j, 3)
                taps = conv(j)
                softmax_max(j, 5)
                attn_lo(j, 0)
                softmax_norm(j, 4)
                next(taps)
                split_unit(unit(MIX0, j, 6) if not last else unit(FFN2_0, 0, 0))
                softmax_max(j, 6)
                next(taps)
                softmax_norm(j, 5)
                next(taps)
                softmax_max(j, 7)
                softmax_norm(j, 6)
                conv_gate(j)
                softmax_norm(j, 7)
                product_lo(PROD_MIX + j, 1)
                split_unit(unit(MIX0, j, 7) if not last else unit(FFN2_0, 0, 1))
                attn_lo(j, 1)
                if not last:
                    for n in range(4):
                        add_y(CHUNK_MIX + j, n, 1 if j == 0 else None)
                    rope(q_t, 2 + j)
                    for n in range(4, TT):
                        add_y(CHUNK_MIX + j, n, 1 if j == 0 else None)
                    split_down(CHUNK_MIX + j + 1)
            ln_turn(2, CHUNK_MIX + PAIRS - 1)

            gate_diagonal(2)
            scale_rows(2)

            def odd_residuals():
                for n in range(1, TT, 2):
                    residual(2, n)

            ffn_body(1, 0, first=True, after_up=odd_residuals)
            with dve.Fori(1, FC - 1) as c:
                ffn_body(1, c)
            ffn_body(1, FC - 1, last=True)
            dve.wait_ge(s_ow, 64)
            for n in range(TT + 1):
                if n < TT:
                    statistics(2, CHUNK_FFN2 + FC - 1, n)
                else:
                    invert(2, TT - 1)
                if n > 0 and n % 2:
                    dve.wait_ge(s_norm, 16 + n)
                    dve.tensor_tensor(y[:, n - 1, :], y[:, n - 1, :], out_g_row, ALU.mult).then_inc(s_og, 1)

        @block.gpsimd
        def _(pool):
            def gate_down(q):
                for i in range(2):
                    pool.wait_ge(s_rawd[i], 32 * q + 32)
                    pool.tensor_tensor(raw_down[:, i, :], raw_down[:, i, :], gate_row, ALU.mult
                                       ).then_inc(s_dgate, 1)

            def residual(stage, n):
                pool.wait_ge(s_tr, 16 * stage + 8 * (n // 4) + 8)
                pool.tensor_tensor(y[:, n, :], y[:, n, :], ln_g_row, ALU.mult).then_inc(s_rm, 1)
                pool.wait_ge(s_rm, 4 * (stage - 1) + n // 2 + 1)
                pool.tensor_tensor(y[:, n, :], y[:, n, :], ln_b_row, ALU.add).then_inc(s_res, 1)

            def row_scale(ln, n):
                s = ln_s[:, n % 2, :]
                m = TT * ln + n
                count = [5 * m]

                def step(ins):
                    ins.then_inc(s_newton, 1)
                    count[0] += 1
                    pool.wait_ge(s_newton, count[0])
                pool.wait_ge(s_rcp, m + 1)
                step(pool.tensor_tensor(s[:, 17:18], s[:, 16:17], s[:, 16:17], ALU.mult))
                step(pool.tensor_tensor(s[:, 18:19], s[:, 17:18], s[:, 14:15], ALU.mult))
                step(pool.tensor_scalar(s[:, 19:20], s[:, 18:19], -0.5, 1.5, ALU.mult, ALU.add))
                step(pool.tensor_tensor(s[:, 20:21], s[:, 16:17], s[:, 19:20], ALU.mult))
                step(pool.tensor_tensor(s[:, 22:23], s[:, 12:13], s[:, 20:21], ALU.mult))
                pool.tensor_scalar(s[:, 21:22], s[:, 22:23], -1.0, None, ALU.mult).then_inc(s_stat, 1)

            pool.memset(cos_t, 1.0).then_inc(s_rbase, 1)
            pool.memset(sin_t, 0.0).then_inc(s_rbase, 1)
            pool.wait_ge(s_gate, 1)
            gate_down(0)
            with pool.Fori(1, FC) as c:
                gate_down(c)
            for stage, q in ((1, CHUNK_MIX), (2, CHUNK_FFN2)):
                for n in range(TT):
                    row_scale(stage - 1, n)
                if stage == 1:
                    pool.memset(q_swap, 0.0).then_inc(s_zero, 1)
                pool.wait_ge(s_rowsc, 2 * stage)
                for n in range(0, TT, 2):
                    residual(stage, n)
                pool.wait_ge(s_gate, stage + 1)
                gate_down(q)
                if stage == 1:
                    for j in range(1, PAIRS):
                        gate_down(q + j)
            with pool.Fori(1, FC) as c:
                gate_down(CHUNK_FFN2 + c)

            def out_row(n):
                if n % 2:
                    pool.wait_ge(s_norm, 16 + n + 1)
                    pool.tensor_tensor(y[:, n, :], y[:, n, :], out_g_row, ALU.mult).then_inc(s_ogp, 1)
                    pool.wait_ge(s_ogp, n // 2 + 1)
                else:
                    pool.wait_ge(s_og, n // 2 + 1)
                pool.tensor_tensor(y[:, n, :], y[:, n, :], out_b_row, ALU.add).then_inc(s_oa, 1)

            for n in range(TT + 1):
                if n < TT:
                    row_scale(2, n)
                if n > 0:
                    out_row(n - 1)


def constants():
    q, k = np.arange(P)[:, None], np.arange(2 * P)[None, :]
    lag = q + P - k
    mask = np.where((lag >= 0) & (lag < P), 0.0, MASKED).astype(np.float32)
    freq = THETA ** (-2.0 * (np.arange(P) // 16) / ROT)
    return {"ident": np.eye(P, dtype=np.float32), "ones": np.ones((P, P), np.float32), "mask": mask,
            "rope_c": freq[:, None].astype(np.float32)}


def kernel(**inputs):
    import concourse.bacc as bacc
    from concourse.bass_utils import run_bass_kernel_spmd

    nc = bacc.Bacc("TRN2", target_bir_lowering=False, num_devices=1)
    arrays = {}
    for name, a in inputs.items():
        a = np.ascontiguousarray(a)
        arrays[name] = a if name == "c" else a[0]
    arrays.update(constants())
    handles = {name: nc.dram_tensor(name + "_dram", a.shape, mybir.dt.from_np(a.dtype), kind="ExternalInput").ap()
               for name, a in arrays.items()}
    out = nc.dram_tensor("out_dram", (SEQ, D), F32, kind="ExternalOutput").ap()
    build(nc, handles, out)
    r = run_bass_kernel_spmd(nc, [{name + "_dram": a for name, a in arrays.items()}], core_ids=[0])
    return r.results[0]["out_dram"].reshape(1, SEQ, D)
```

```python
from contextlib import ExitStack

import numpy as np

import concourse.bass as bass
import concourse.mybir as mybir
from concourse.alu_op_type import AluOpType as ALU

F32 = mybir.dt.float32
F32R = mybir.dt.float32r
I32 = mybir.dt.int32
ACT = mybir.ActivationFunctionType
AXX = mybir.AxisListType.X

P = 128
D = 1024
SEQ = 1024
KT = D // P
TT = SEQ // P
HALF = 512
D_FF = 2816
FC = D_FF // (2 * P)
HEAD_DIM = 64
N_HEADS = 8
PAIRS = N_HEADS // 2
ATTN_W = 512
CONV_W = 512
KV_W = 128
U0 = ATTN_W + 2 * KV_W
BG0 = U0 + CONV_W
CG0 = BG0 + CONV_W
ROT = 16
THETA = 500000.0
LN_EPS = 1e-5
ALPHA = 2.0 ** 0.25
SCALE = HEAD_DIM ** -0.5
MASKED = -1.0e30
N_MOD = 9
STRIPS = N_MOD * D // HALF
STRIPS_BEFORE = STRIPS - FC
PI = float(np.pi)

UNITS_FFN = 4 * FC
MIX0 = UNITS_FFN
FFN2_0 = MIX0 + 2 + 4 * PAIRS
CHUNK_MIX = FC
CHUNK_FFN2 = FC + PAIRS
PROD_MIX = 2 * FC
PROD_FFN2 = PROD_MIX + PAIRS

COL_C = 0
COL_LN = 8
COL_BADA = 40
COL_CONV = 112
N_COLS = 124

TWO_PI_1 = 6.28125
TWO_PI_2 = float(np.round((2 * np.pi - TWO_PI_1) * 2.0 ** 21) / 2.0 ** 21)
TWO_PI_3 = float(2 * np.pi - TWO_PI_1 - TWO_PI_2)
ROUND_1 = 1.5 * 2.0 ** 23
ROUND_2K = 1.5 * 2.0 ** 34
ROPE_STEPS = 19
OUT_VECTOR = (0, 1, 5, 6, 7)
OUT_POOL = (2, 3, 4)
OUT_ORDER = (0, 1, 2, 3, 4, 5, 6, 7)


def unit(base, c, k):
    return base + 4 * c + k, base // 2 + 2 * c + k // 2, k % 2


def pool_splits(n):
    return n % (2 * KT) in (1, 5, 10, 13)


POOL_TILES = sum(pool_splits(n) for n in range(2 * KT))


def build(nc, t, out):
    with ExitStack() as ctx:
        def sb(name, shape, dt=F32):
            return ctx.enter_context(nc.sbuf_tensor(name, shape, dt))

        def sem(name):
            return ctx.enter_context(nc.semaphore(name))

        h_hi = sb("h_hi", [P, KT, SEQ], F32R)
        h_lo = sb("h_lo", [P, KT, SEQ], F32R)
        act_hi = sb("act_hi", [P, 2, SEQ], F32R)
        act_lo = sb("act_lo", [P, 2, SEQ], F32R)
        wu_hi = sb("wu_hi", [P, 2, D], F32R)
        wu_lo = sb("wu_lo", [P, 2, D], F32R)
        wd_hi = sb("wd_hi", [P, 2, D], F32R)
        wd_lo = sb("wd_lo", [P, 2, D], F32R)
        y = sb("y", [P, TT, D])
        raw_unit = sb("raw_unit", [P, 2, D])
        raw_down = sb("raw_down", [P, 2, D])
        arena = sb("arena", [P, 11, D])
        cos_t, sin_t, sg, prod, gate_row, k_t, v_tok, q_t, q_swap = (arena[:, i, :] for i in range(9))
        strip = arena[:, 7:11, :].rearrange("p a (b n) -> p (a b) n", n=HALF)
        scores = arena[:, 9, :].rearrange("p (s h k) -> p s h k", s=2, h=2)
        probsT = arena[:, 10, :].rearrange("p (s k h q) -> p s k h q", s=2, k=2, h=2)
        early_strips = {1: (raw_down[:], arena[:, 2:4, :]), 2: (arena[:, 0:2, :], y[:, 6:8, :])}
        strip_acc = [k_t[:, 0:HALF], k_t[:, HALF:]]
        h_tmp = [v_tok[:, 0:HALF], v_tok[:, HALF:], sg[:, 0:HALF], k_t[:, 0:HALF]]
        diag = v_tok
        const_rows = gate_row[0:N_COLS, 0:P]
        v_blk = v_tok.rearrange("p (b n) -> p b n", b=TT)
        rope_w = v_tok[:, 0:5 * SEQ // 16].rearrange("p (s n) -> p s n", n=SEQ // 16)
        ln_g_row, ln_b_row = arena[:, 9, :], arena[:, 10, :]
        out_g_row, out_b_row = q_t, q_swap
        mask = sb("mask", [P, 2 * P])
        ident = sb("ident", [P, P])
        ones = sb("ones", [P, P])
        rope_c = sb("rope_c", [P, 1])
        cols = sb("cols", [P, N_COLS])
        cond = sb("cond", [P, KT])
        mod = sb("mod", [P, 8 * N_MOD])
        mod_sum = sb("mod_sum", [P, HALF // P])
        affine = sb("affine", [P, 3, 2, KT])
        gate_c = sb("gate_c", [P, KT])
        sink = sb("sink", [P, 2, PAIRS])
        neg_sink = sb("neg_sink", [P, 2, PAIRS])
        eps = sb("eps", [P, 1])
        ln_s = sb("ln_s", [P, 4, 24])
        at_s = sb("at_s", [P, 2, 16])

        ps_unit = [ctx.enter_context(nc.psum_tensor(f"ps_unit{i}", [P, 2, HALF], F32)) for i in range(2)]
        ps_down = [ctx.enter_context(nc.psum_tensor(f"ps_down{i}", [P, 2, HALF], F32)) for i in range(2)]
        ps_mod = ps_down[1][:, 0, :]
        ps_score = ps_down[0]
        ps_probsT = ps_down[1][:, 0, :].rearrange("p (k h q) -> p k h q", k=2, h=2)
        ps_attn = ps_down[1][:, 1, :]

        def flat(p):
            return p[:].rearrange("p a b -> p (a b)")

        s_const = sem("const_rows_loaded")
        s_ones = sem("ones_and_mask_loaded")
        s_sink = sem("sink_loaded")
        s_x = [sem(f"x_loaded{i}") for i in range(2)]
        s_colsT = sem("cols_transposed")
        s_cols = sem("cols_copied")
        s_cond = sem("cond_ready")
        s_strip = [sem(f"strip_loaded{i}") for i in range(2)]
        s_strip_early = {n: [sem(f"strip{n}_loaded{i}") for i in range(2)] for n in (1, 2)}
        s_acc = sem("strip_products")
        s_modmm = sem("mod_turned")
        s_modsum = sem("mod_summed")
        s_mod = sem("mod_ready")
        s_aff = sem("affine_ready")
        s_diag = sem("gate_diagonal")
        s_gatemm = sem("gate_spread")
        s_gate = sem("gate_row_ready")
        s_rawu = [sem(f"unit_weights_loaded{i}") for i in range(2)]
        s_whi = sem("unit_weights_hi")
        s_wlo = sem("unit_weights_split")
        s_unit = sem("unit_done")
        s_uhalf = sem("last_units_first_half_done")
        s_silu = sem("silu_first_half_ready")
        s_pfree = [sem(f"unit_psum_read{i}") for i in range(2)]
        s_rawd = [sem(f"down_weights_loaded{i}") for i in range(2)]
        s_dgate = sem("down_weights_gated")
        s_dhi = sem("down_weights_hi")
        s_dlo = sem("down_weights_split")
        s_prod = sem("product_ready")
        s_phi = sem("product_hi")
        s_act = [sem(f"act_ready{i}") for i in range(2)]
        s_down = sem("down_tile_done")
        s_y = sem("y_added")
        s_ln = sem("ln_steps")
        s_var = sem("variance_ready")
        s_std = sem("deviation_ready")
        s_stat = sem("ln_scale_ready")
        s_norm = sem("rows_normalised")
        s_tr = sem("rows_transposed")
        s_ev = sem("h_affine_done")
        s_hhi = sem("h_hi_ready")
        s_rcp = sem("deviation_inverted")
        s_eps = sem("eps_ready")
        s_nsink = sem("neg_sink_ready")
        s_newton = sem("newton_steps")
        s_resd = sem("residual_ready_vector")
        s_rmd = sem("residual_scaled_vector")
        s_h = sem("h_ready_vector")
        s_hp = sem("h_ready_gpsimd")
        s_rows = sem("ln_rows_loaded")
        s_rowsc = sem("ln_rows_scaled")
        s_rm = sem("residual_scaled")
        s_res = sem("residual_ready")
        s_pos = sem("positions_loaded")
        s_rt = sem("rope_table_steps")
        s_sin = sem("sines_ready")
        s_rtab = sem("rope_values_ready")
        s_rbase = sem("rope_tables_filled")
        s_rdram = sem("rope_values_stored")
        s_rload = sem("rope_tables_loaded")
        s_zero = sem("swap_zeroed")
        s_swap = sem("rotary_rows_swapped")
        s_rs = sem("rope_steps")
        s_rope = sem("rope_done")
        s_vT = sem("v_transposed")
        s_v = sem("v_ready")
        s_conv = sem("conv_steps")
        s_sc = sem("scores_ready")
        s_sm = sem("softmax_steps")
        s_msk = sem("scores_masked")
        s_max = sem("maximum_ready")
        s_exp = sem("exponentials_ready")
        s_p = sem("probs_ready")
        s_pT = sem("probs_transposed")
        s_pTc = sem("probsT_copied")
        s_pv = sem("values_summed")
        s_ahi = sem("attention_hi")
        s_ow = sem("out_affine_loaded")
        s_og = sem("out_gained")
        s_ogp = sem("out_gained_gpsimd")
        s_oa = sem("out_rows_ready_gpsimd")
        s_on = sem("out_rows_ready_vector")
        s_out = sem("out_stored")

        const_loads = ((const_rows[COL_C:COL_LN, :], t["c"].rearrange("a (r n) -> (a r) n", n=P)),
                       (ident[:], t["ident"][:, :]),
                       (const_rows[8:16, :], t["ln1_g"].rearrange("(r n) -> r n", n=P)),
                       (const_rows[16:24, :], t["ln1_b"].rearrange("(r n) -> r n", n=P)),
                       (const_rows[24:32, :], t["ln2_g"].rearrange("(r n) -> r n", n=P)),
                       (const_rows[32:40, :], t["ln2_b"].rearrange("(r n) -> r n", n=P)),
                       (const_rows[COL_BADA:COL_CONV, :], t["b_ada"].rearrange("(r n) -> r n", n=P)),
                       (const_rows[COL_CONV:N_COLS, :], t["conv_w"].rearrange("a (r n) -> (a r) n", n=P)))
        w_gu = [t["ffn1_w_gate_up"], t["ffn2_w_gate_up"]]
        w_dn = [t["ffn1_w_down"], t["ffn2_w_down"]]
        rope_dram = nc.dram_tensor("rope_values", (3, P, SEQ // 16), F32, kind="Internal").ap()
        block = ctx.enter_context(nc.Block())

        def rows_psum(n):
            if n // KT % 2:
                return ps_down[1][:, n % 2, :]
            return ps_unit[n % 2][:, 0 if n // KT == 2 else 1, :]

        def await_h(eng, n):
            on_gpsimd = sum(pool_splits(m) for m in range(n + 1))
            if pool_splits(n):
                eng.wait_ge(s_hp, on_gpsimd)
            else:
                eng.wait_ge(s_h, n + 1 - on_gpsimd)

        def await_stage_h(eng, stage):
            eng.wait_ge(s_hp, POOL_TILES * (stage + 1))
            eng.wait_ge(s_h, (2 * KT - POOL_TILES) * (stage + 1))

        def is_early(n):
            return isinstance(n, int) and n in early_strips

        def strip_part(n, i):
            if is_early(n):
                return early_strips[n][i].rearrange("p a (b n) -> p (a b) n", n=HALF)
            return strip[:, 4 * i:4 * i + 4, :]

        def acc_of(n):
            return strip_acc[n % 2 if isinstance(n, int) and n < STRIPS_BEFORE else 1]

        @block.sync
        def _(sp):
            def wait_place(sem_, value):
                if not isinstance(value, int):
                    value = sp.to_reg(value)
                    sp.wait_ge(s_sink, 16)
                sp.wait_ge(sem_, value)

            def load_strip(n):
                for i in range(2):
                    if isinstance(n, int) and n <= 3:
                        free = None if n < 3 else 4 + 4 * i
                    else:
                        free = sp.snap(8 * n - 4 + 4 * i)
                    src = t["w_ada"][HALF * i:HALF * (i + 1), bass.ds(HALF * n, HALF)]
                    if free is not None:
                        wait_place(s_acc, free)
                    loaded = s_strip_early[n] if is_early(n) else s_strip
                    sp.dma_start(strip_part(n, i), src.rearrange("(k p) n -> p k n", p=P)
                                 ).then_inc(loaded[i], 16)

            def unit_columns(n, c, k):
                if isinstance(n, int) and MIX0 <= n < FFN2_0:
                    j, kind = divmod(n - MIX0 - 3, 4)
                    if n == MIX0:
                        col = ATTN_W
                    elif n == MIX0 + 2:
                        col = ATTN_W + KV_W
                    elif n == MIX0 + 1 or kind == 3:
                        j = 0 if n == MIX0 + 1 else j + 1
                        for h in range(2):
                            col = HEAD_DIM * (j + PAIRS * h)
                            yield (raw_unit[:, k % 2, :].rearrange("p (k h n) -> p h k n", k=KT, h=2)[:, h],
                                   t["w_in"][:, col:col + HEAD_DIM].rearrange("(k p) n -> p k n", p=P))
                        return
                    else:
                        col = (U0, CG0, BG0)[kind] + P * j
                    w = t["w_in"]
                else:
                    w = w_gu[c[0]]
                    col = (0, D_FF, P, D_FF + P)[k] + 2 * P * c[1]
                for i in range(2):
                    yield (raw_unit[:, k % 2, HALF * i:HALF * (i + 1)].rearrange("p (k n) -> p k n", n=P),
                           w[HALF * i:HALF * (i + 1), bass.ds(col, P)].rearrange("(k p) n -> p k n", p=P))

            def load_unit(n, c, k):
                pieces = list(unit_columns(n, c, k))
                if not (isinstance(n, int) and n < 2):
                    wait_place(s_wlo, sp.snap(n - 1))
                for dst, src in pieces:
                    sp.dma_start(dst, src).then_inc(s_rawu[k % 2], 16)

            def load_down(q, i, src0, src1):
                free = None if isinstance(q, int) and q == 0 else sp.snap(2 * q + i - 1)
                srcs = [w[bass.ds(r, 64), :] for w, r in (src0, src1)]
                if free is not None:
                    wait_place(s_dlo, free)
                for m, src in enumerate(srcs):
                    sp.dma_start(raw_down[64 * m:64 * m + 64, i, :], src).then_inc(s_rawd[i], 16)

            def load_down_ffn(f, c):
                q = (0, CHUNK_FFN2)[f] + c
                for i in range(2):
                    r = 2 * P * c + P * i
                    load_down(q, i, (w_dn[f], r), (w_dn[f], r + 64))

            def load_down_mix(j):
                load_down(CHUNK_MIX + j, 0, (t["w_out"], HEAD_DIM * j), (t["w_out"], HEAD_DIM * (PAIRS + j)))
                load_down(CHUNK_MIX + j, 1, (t["w_out"], ATTN_W + P * j), (t["w_out"], ATTN_W + P * j + 64))

            def ffn_body(f, c, strip_n=None):
                base = (0, FFN2_0)[f]
                load_unit(base + 4 * c + 4, (f, c + 1), 0)
                if strip_n is not None:
                    load_strip(strip_n)
                load_unit(base + 4 * c + 5, (f, c + 1), 1)
                load_unit(base + 4 * c + 6, (f, c + 1), 2)
                load_down_ffn(f, c + 1)
                load_unit(base + 4 * c + 7, (f, c + 1), 3)

            def load_x(half):
                for n in range(4 * half, 4 * half + 4):
                    sp.dma_start(y[:, n, :], t["x"][P * n:P * n + P, :]).then_inc(s_x[half], 16)

            for dst, src in const_loads[0::2]:
                sp.dma_start(dst, src).then_inc(s_const, 16)
            load_strip(0)
            load_strip(1)
            load_strip(2)
            sp.dma_start(sink[:].rearrange("p h j -> p (h j)"),
                         t["attn_sinks"].partition_broadcast(P)).then_inc(s_sink, 16)
            load_strip(3)
            load_unit(0, (0, 0), 0)
            load_x(0)
            load_unit(1, (0, 0), 1)
            sp.wait_ge(s_acc, 8 * 3)
            load_x(1)
            load_unit(2, (0, 0), 2)
            load_strip(4)
            load_unit(3, (0, 0), 3)
            load_down_ffn(0, 0)
            load_unit(4, (0, 1), 0)
            load_strip(5)
            load_unit(5, (0, 1), 1)
            load_strip(6)
            load_unit(6, (0, 1), 2)
            load_strip(7)
            load_down_ffn(0, 1)
            load_unit(7, (0, 1), 3)
            with sp.Fori(1, FC - 1) as c:
                ffn_body(0, c, STRIPS_BEFORE + c)
            sp.wait_ge(s_gatemm, 1)
            for f in range(ROT // 2):
                sp.dma_start(rope_w[16 * f:16 * f + 16, 0, :].bitcast(I32),
                             t["positions"].rearrange("(b n) -> b n", b=16)).then_inc(s_pos, 16)
            load_strip(STRIPS - 1)
            load_unit(MIX0, None, 0)
            load_unit(MIX0 + 1, None, 1)
            load_down_mix(0)
            sp.wait_ge(s_acc, 8 * STRIPS)
            sp.dma_start(ln_g_row, t["ln1_g"].partition_broadcast(P)).then_inc(s_rows, 16)
            sp.dma_start(ln_b_row, t["ln1_b"].partition_broadcast(P)).then_inc(s_rows, 16)
            sp.wait_ge(s_rtab, 1)
            sp.wait_ge(s_sin, 2)
            for i, w in enumerate((3, 2, 4)):
                sp.dma_start(rope_dram[i], rope_w[:, w, :]).then_inc(s_rdram, 16)
            sp.wait_ge(s_rdram, 48)
            sp.wait_ge(s_rbase, 2)
            for h in (0, 64):
                for row, dst, i in ((h, cos_t, 0), (h + 8, cos_t, 0), (h, sin_t, 2), (h + 8, sin_t, 1)):
                    sp.dma_start(dst[row:row + 8, :], rope_dram[i].rearrange("(f b) n -> f (b n)", b=16)
                                 ).then_inc(s_rload, 16)
            load_unit(MIX0 + 2, None, 0)
            load_unit(MIX0 + 3, None, 1)
            for j in range(PAIRS):
                n = MIX0 + 4 * j + 4
                load_unit(n, None, 0)
                load_unit(n + 1, None, 1)
                if j + 1 < PAIRS:
                    load_unit(n + 2, None, 0)
                    load_down_mix(j + 1)
                    load_unit(n + 3, None, 1)
            load_unit(FFN2_0, (1, 0), 0)
            load_unit(FFN2_0 + 1, (1, 0), 1)
            load_down_ffn(1, 0)
            sp.wait_ge(s_pv, TT * PAIRS)
            sp.dma_start(ln_g_row, t["ln2_g"].partition_broadcast(P)).then_inc(s_rows, 16)
            sp.dma_start(ln_b_row, t["ln2_b"].partition_broadcast(P)).then_inc(s_rows, 16)
            sp.dma_start(out_g_row, t["ln3_g"].partition_broadcast(P)).then_inc(s_ow, 32)
            sp.dma_start(out_b_row, t["ln3_b"].partition_broadcast(P)).then_inc(s_ow, 32)
            load_unit(FFN2_0 + 2, (1, 0), 2)
            load_unit(FFN2_0 + 3, (1, 0), 3)
            ffn_body(1, 0)
            with sp.Fori(1, FC - 1) as c:
                ffn_body(1, c)
            for n in OUT_ORDER:
                if n in OUT_POOL:
                    sp.wait_ge(s_oa, OUT_POOL.index(n) + 1)
                else:
                    sp.wait_ge(s_on, OUT_VECTOR.index(n) + 1)
                sp.dma_start(out[P * n:P * n + P, :], y[:, n, :]).then_inc(s_out, 16)
            sp.wait_ge(s_out, 16 * TT)

        @block.tensor
        def _(pe):
            def three(ps, st_hi, st_lo, mv_hi, mv_lo, first, last):
                n = len(ps)
                for i in range(n):
                    pe.matmul(ps[i], st_hi, mv_hi[i], start=first, stop=False)
                for i in range(n):
                    pe.matmul(ps[i], st_hi, mv_lo[i], start=False, stop=False)
                for i in range(n):
                    mm = pe.matmul(ps[i], st_lo, mv_hi[i], start=False, stop=last)
                return mm

            def halves(x):
                return [x[:, HALF * i:HALF * (i + 1)] for i in range(2)]

            def unit_kstep(par, k, parts=(0, 1)):
                w = slice(P * k, P * k + P)
                ps = [ps_unit[par][:, i, :] for i in parts]
                hi = [halves(h_hi[:, k, :])[i] for i in parts]
                lo = [halves(h_lo[:, k, :])[i] for i in parts]
                return three(ps, wu_hi[:, par, w], wu_lo[:, par, w], hi, lo, k == 0, k == KT - 1)

            def begin_unit(u):
                n, before, par = u
                pe.wait_ge(s_wlo, n + 1)
                if not (isinstance(before, int) and before == 0):
                    pe.wait_ge(s_pfree[par], before)

            def run_unit(u, beside=()):
                begin_unit(u)
                for k in range(KT):
                    mm = unit_kstep(u[2], k)
                    if k == KT - 1:
                        mm.then_inc(s_unit, 1)
                    if k < len(beside) and beside[k]:
                        beside[k]()

            def down_part(q, n, i, mods=None):
                if n == 0:
                    pe.wait_ge(s_dlo, 2 * q + i + 1)
                if n % 4 == 0:
                    pe.wait_ge(s_act[i], 2 * q + n // 4 + 1)
                if i == 0 and n == 1 and isinstance(q, int) and CHUNK_MIX <= q < CHUNK_FFN2:
                    pe.wait_ge(s_act[0], 2 * q + 2)
                if i == 0 and not (isinstance(q, int) and q == 0 and n < 2):
                    pe.wait_ge(s_y, 8 * q + n - 1)
                if i == 0 and n == 1 and mods is not None:
                    pe.wait_ge(s_mod, mods)
                ps = [ps_down[n % 2][:, m, :] for m in range(2)]
                tok = slice(P * n, P * n + P)
                return three(ps, act_hi[:, i, tok], act_lo[:, i, tok], halves(wd_hi[:, i, :]),
                             halves(wd_lo[:, i, :]), i == 0, i == 1)

            def down_all(q, tiles=range(TT), mods=None, late=False):
                tiles = list(tiles)
                if late:
                    for n in tiles[:2]:
                        down_part(q, n, 0, mods)
                    for n in tiles[:2]:
                        down_part(q, n, 1).then_inc(s_down, 1)
                    tiles = tiles[2:]
                for n in tiles:
                    down_part(q, n, 0, mods)
                    down_part(q, n, 1).then_inc(s_down, 1)

            def transpose_rows(stage, half, d):
                if stage == 0:
                    pe.wait_ge(s_x[half], 64)
                else:
                    pe.wait_ge(s_norm, 8 * (stage - 1) + 4 * half + 4)
                n = 16 * stage + 8 * half + d
                if d == 0:
                    if half:
                        if stage:
                            pe.wait_ge(s_y, 8 * (0, FC, CHUNK_FFN2)[stage])
                        else:
                            pe.wait_ge(s_mod, 4)
                    elif stage == 1:
                        pe.wait_ge(s_silu, 1)
                        pe.wait_ge(s_prod, PROD_MIX)
                    elif stage == 2:
                        for free in s_pfree:
                            pe.wait_ge(free, FFN2_0 // 2)
                if n >= 2:
                    pe.wait_ge(s_ev, n - 1)
                for i in range(4):
                    mm = pe.transpose(rows_psum(n)[:, P * i:P * i + P],
                                      y[:, 4 * half + i, P * d:P * d + P], ident[:])
                mm.then_inc(s_tr, 1)

            def first_units(stage, base):
                u = [unit(base, 0, k) for k in range(2)]
                steps = [(half, d) for half in range(2) for d in range(KT)]
                h0 = 2 * KT * stage

                def turn_and_step(turns, i):
                    if i < turns:
                        transpose_rows(stage, *steps[i])
                    half, d = steps[i - 3]
                    await_h(pe, h0 + i - 3)
                    return unit_kstep(0, d, (half,))

                begin_unit(u[0])
                if stage == 1:
                    pe.wait_ge(s_ev, h0 + KT)
                else:
                    transpose_rows(stage, *steps[2])
                if stage == 0:
                    for i in range(3, len(steps) + 3):
                        mm = turn_and_step(len(steps), i)
                    mm.then_inc(s_unit, 1)
                    pe.wait_ge(s_ev, h0 + 2 * KT)
                    run_unit(u[1])
                    return
                for i in range(3, KT + 3):
                    turn_and_step(0 if stage == 1 else KT, i)
                begin_unit(u[1])
                pe.wait_ge(s_ev, h0 + KT)
                for k in range(KT):
                    unit_kstep(1, k, (0,))
                for i in range(KT, KT + 3):
                    transpose_rows(stage, *steps[i])
                for i in range(KT + 3, len(steps) + 3):
                    mm = turn_and_step(len(steps), i)
                mm.then_inc(s_unit, 1)
                for k in range(KT):
                    mm = unit_kstep(1, k, (1,))
                mm.then_inc(s_unit, 1)
                pe.wait_ge(s_ev, h0 + 2 * KT)

            def down_and_turn(q, stage):
                down_all(q, range(TT - 1), late=True)
                transpose_rows(stage, 0, 0)
                transpose_rows(stage, 0, 1)
                down_all(q, (TT - 1,))

            def sum_strip(n, q=0):
                pe.wait_ge(s_acc, 8 * n + 8)
                if not isinstance(n, int) or n > 0:
                    pe.wait_ge(s_mod, n)
                if not isinstance(q, int) or q > 0:
                    pe.wait_ge(s_y, 8 * q)
                for i in range(4):
                    mm = pe.transpose(ps_mod[:, P * i:P * i + P], acc_of(n)[:, P * i:P * i + P], ident[:])
                mm.then_inc(s_modmm, 1)

            def spread_gate(stage, q):
                pe.wait_ge(s_ones, 16 * 3)
                pe.wait_ge(s_diag, stage + 1)
                if q > 0:
                    pe.wait_ge(s_y, 8 * q)
                for d in range(KT):
                    mm = pe.matmul(ps_down[0][:, d // 4, P * (d % 4):P * (d % 4) + P], ones[:],
                                   diag[:, P * d:P * d + P], start=True, stop=True)
                mm.then_inc(s_gatemm, 1)

            def ffn_body(f, c, strip_n=None, beside=((), (), ()), late_sum=False):
                base, q0 = ((0, 0), (FFN2_0, CHUNK_FFN2))[f]
                if not (isinstance(c, int) and c == 0):
                    run_unit(unit(base, c, 1))
                run_unit(unit(base, c, 2), beside[0])
                run_unit(unit(base, c, 3), beside[1])
                run_unit(unit(base, c, 4), beside[2])
                if late_sum:
                    down_all(q0 + c, mods=strip_n)
                    sum_strip(strip_n, q0 + c + 1)
                    return
                if strip_n is not None:
                    sum_strip(strip_n, q0 + c)
                down_all(q0 + c, mods=None if strip_n is None else strip_n + 1)

            def last_chunk(f):
                base, q = ((0, FC - 1), (FFN2_0, CHUNK_FFN2 + FC - 1))[f]
                run_unit(unit(base, FC - 1, 1))
                for g in range(2):
                    for kind in (2, 3):
                        u = unit(base, FC - 1, kind)
                        if g == 0:
                            begin_unit(u)
                        for k in range(KT):
                            mm = unit_kstep(u[2], k, (g,))
                            if k == KT - 1:
                                mm.then_inc((s_uhalf, s_unit)[g], 1)
                            if f == 0 and kind == 2 and g == 0 and k == KT - 2:
                                sum_strip(STRIPS - 1, q)
                            if f == 0 and kind == 3 and g == 1 and k >= KT - 3:
                                transpose_rows(1, 0, k - (KT - 3))
                    if g == 0 or f == 1:
                        down_all(q, range(4 * g, 4 * g + 4), STRIPS if f == 0 else None, late=True)
                    else:
                        turns = iter(range(3, KT))
                        for i in range(2):
                            for n in (4, 5):
                                mm = down_part(q, n, i)
                                if i == 1:
                                    mm.then_inc(s_down, 1)
                                transpose_rows(1, 0, next(turns))
                        down_all(q, (6,))
                        transpose_rows(1, 0, next(turns))
                        down_all(q, (7,))

            pe.wait_ge(s_const, 16 * len(const_loads))
            pe.transpose(ps_unit[0][:, 0, 0:N_COLS], const_rows, ident[0:N_COLS, 0:N_COLS]
                         ).then_inc(s_colsT, 1)
            for n in range(4):
                sum_strip(n)
            transpose_rows(0, 0, 0)
            transpose_rows(0, 0, 1)
            pe.wait_ge(s_cols, 1)
            first_units(0, 0)

            ffn_body(0, 0, 7, ((None,) * 7 + (lambda: sum_strip(4),), (None,) * 7 + (lambda: sum_strip(5),),
                               (None, lambda: spread_gate(0, 0), *(None,) * 5, lambda: sum_strip(6))),
                     late_sum=True)
            with pe.Fori(1, FC - 1) as c:
                ffn_body(0, c, STRIPS_BEFORE + c)
            last_chunk(0)

            first_units(1, MIX0)
            spread_gate(1, FC)
            run_unit(unit(MIX0, 0, 2))

            def turn_v():
                pe.wait_ge(s_pfree[0], MIX0 // 2 + 2)
                for b in range(TT):
                    mm = pe.transpose(ps_unit[0][:, b // 4, P * (b % 4):P * (b % 4) + P],
                                      sg[:, P * b:P * b + P], ident[:])
                mm.then_inc(s_vT, 1)

            def score(j, b):
                n = TT * j + b
                if b == 0:
                    pe.wait_ge(s_rope, 2 + j)
                    pe.wait_ge(s_y, 8 * (CHUNK_MIX + j))
                    if j == 0:
                        pe.wait_ge(s_gate, 2)
                if n >= 1:
                    pe.wait_ge(s_msk, n)
                k0 = P * (b - 1) if b else 0
                for h in range(2):
                    r = slice(64 * h, 64 * h + 64)
                    o0 = 256 * (b % 2)
                    mm = pe.matmul(ps_score[:, h, o0 + (0 if b else P):o0 + 256], q_t[r, P * b:P * b + P],
                                   k_t[r, k0:P * b + P], start=True, stop=True)
                mm.then_inc(s_sc, 1)

            def turn_probs(j, b):
                n = TT * j + b
                pe.wait_ge(s_p, n + 1)
                if n >= 1:
                    pe.wait_ge(s_pTc, n)
                for k in range(0 if b else 1, 2):
                    for h in range(2):
                        mm = pe.transpose(ps_probsT[:, k, h, :], scores[:, b % 2, h, P * k:P * k + P],
                                          ident[:])
                mm.then_inc(s_pT, 1)

            def values(j, b):
                n = TT * j + b
                pe.wait_ge(s_pTc, n + 1)
                if n == 0:
                    pe.wait_ge(s_v, 1)
                if b % 4 == 0 and n >= 4:
                    pe.wait_ge(s_act[0], 2 * CHUNK_MIX + n // 4)
                for h in range(2):
                    for k in range(0 if b else 1, 2):
                        mm = pe.matmul(ps_attn[64 * h:64 * h + 64, P * (b % 4):P * (b % 4) + P],
                                       v_blk[:, b - 1 + k, 64 * h:64 * h + 64], probsT[:, b % 2, k, h, :],
                                       start=k == (0 if b else 1), stop=k == 1)
                mm.then_inc(s_pv, 1)

            for j in range(PAIRS):
                steps = [None] * 32
                for b in range(TT):
                    steps[3 * b] = lambda b=b: score(j, b)
                    steps[3 * b + 4] = lambda b=b: turn_probs(j, b)
                    steps[3 * b + 5] = lambda b=b: values(j, b)
                if j == 0:
                    steps[1] = turn_v
                run_unit(unit(MIX0, j, 3), steps[0:8])
                if j == 0:
                    pe.wait_ge(s_v, 1)
                run_unit(unit(MIX0, j, 4), steps[8:16])
                run_unit(unit(MIX0, j, 5), steps[16:24])
                if j + 1 < PAIRS:
                    run_unit(unit(MIX0, j, 6), steps[24:32])
                    down_all(CHUNK_MIX + j)
                else:
                    for s in steps[24:32]:
                        if s:
                            s()
            down_and_turn(CHUNK_MIX + PAIRS - 1, 2)

            first_units(2, FFN2_0)
            ffn_body(1, 0, beside=((), (lambda: spread_gate(2, CHUNK_FFN2),), ()))
            with pe.Fori(1, FC - 1) as c:
                ffn_body(1, c)
            last_chunk(1)

        @block.scalar
        def _(act):
            def split_unit(u):
                n, before, par = u
                act.wait_ge(s_rawu[par], 32 * before + 32)
                if not (isinstance(n, int) and n < 2):
                    act.wait_ge(s_unit, n - 1)
                act.activation(wu_hi[:, par, :], raw_unit[:, par, :], ACT.Copy).then_inc(s_whi, 1)

            def split_down(q):
                for i in range(2):
                    act.wait_ge(s_dgate, 2 * q + i + 1)
                    if not (isinstance(q, int) and q == 0):
                        act.wait_ge(s_down, 8 * q)
                    act.activation(wd_hi[:, i, :], raw_down[:, i, :], ACT.Copy).then_inc(s_dhi, 1)

            def silu_gate(u):
                n, before, par = u
                act.wait_ge(s_unit, n + 1)
                if not (isinstance(before, int) and before == 0):
                    act.wait_ge(s_pfree[1], before)
                act.activation(sg, flat(ps_unit[par]), ACT.Silu).then_inc(s_pfree[par], 1)

            def h_taken(stage):
                await_stage_h(act, stage)

            def product_hi(m, i, q, u, halves=(0, 1)):
                for g in halves:
                    if g == 0:
                        act.wait_ge(s_prod, m + 1)
                        if not (isinstance(q, int) and q == 0):
                            act.wait_ge(s_down, 8 * q)
                    else:
                        act.wait_ge(s_pfree[1], u[1] + 1)
                    at = slice(HALF * g, HALF * g + HALF)
                    act.activation(act_hi[:, i, at], prod[:, at], ACT.Copy).then_inc(s_phi, 1)

            def h_out(stage, half, d):
                n = 16 * stage + 8 * half + d
                act.wait_ge(s_tr, n + 1)
                act.wait_ge(s_aff, stage + 1)
                if n >= 4:
                    await_h(act, n - 4)
                act.activation(h_tmp[n % 4], rows_psum(n), ACT.Identity,
                               bias=affine[:, stage, 1, d:d + 1], scale=affine[:, stage, 0, d:d + 1]
                               ).then_inc(s_ev, 1)

            def deviation(ln, n):
                m = TT * ln + n
                act.wait_ge(s_eps, 1)
                act.wait_ge(s_var, m + 1)
                act.activation(ln_s[:, n % 4, 15:16], ln_s[:, n % 4, 13:14], ACT.Sqrt, bias=eps[:, 0:1]
                               ).then_inc(s_std, 1)

            def normalise(ln, n):
                m = TT * ln + n
                act.wait_ge(s_stat, m + 1)
                act.activation(y[:, n, :], y[:, n, :], ACT.Identity, bias=ln_s[:, n % 4, 21:22],
                               scale=ln_s[:, n % 4, 20:21]).then_inc(s_norm, 1)

            def last_silu(f, g):
                n, before, par = unit((0, FFN2_0)[f], FC - 1, 2)
                if g == 0:
                    act.wait_ge(s_uhalf, 2 * f + 1)
                    act.wait_ge(s_pfree[1], before)
                else:
                    act.wait_ge(s_unit, n + 1)
                at = slice(HALF * g, HALF * g + HALF)
                act.activation(sg[:, at], ps_unit[par][:, g, :], ACT.Silu).then_inc((s_silu, s_pfree[par])[g], 1)

            def normalise_tiles(ln, tiles, rows):
                deviation(ln, tiles[0])
                for n in tiles:
                    if n + 1 in tiles:
                        deviation(ln, n + 1)
                    if n in rows:
                        normalise(ln, n)

            def last_chunk(f):
                base, q, m = ((0, FC - 1, PROD_MIX - 1), (FFN2_0, CHUNK_FFN2 + FC - 1, PROD_FFN2 + 2 * FC - 1))[f]
                ln = 2 * f
                rows = OUT_POOL if f else None
                split_unit(unit(base, FC - 1, 2))
                split_unit(unit(base, FC - 1, 3))
                product_hi(m - 1, 0, q, unit(base, FC - 1, 1))
                split_down(q)
                last_silu(f, 0)
                if f == 0:
                    rope_sines()
                product_hi(m, 1, q, unit(base, FC - 1, 3), (0,))
                deviation(ln, 0)
                for n in range(4):
                    if n < 3:
                        deviation(ln, n + 1)
                    else:
                        last_silu(f, 1)
                    if rows is None or n in rows:
                        normalise(ln, n)
                if f == 0:
                    split_unit(unit(base, FC, 0))
                    act.wait_ge(s_rdram, 48)
                    for d in range(3):
                        h_out(1, 0, d)
                product_hi(m, 1, q, unit(base, FC - 1, 3), (1,))
                if f:
                    normalise_tiles(ln, range(4, TT), rows)
                    return
                h_out(1, 0, 3)
                h_out(1, 0, 4)
                h_out(1, 0, 5)
                deviation(ln, 4)
                h_out(1, 0, 6)
                for n in range(4, TT):
                    if n == 5:
                        h_out(1, 0, 7)
                        split_unit(unit(base, FC, 1))
                    if n + 1 < TT:
                        deviation(ln, n + 1)
                    normalise(ln, n)
                for d in range(KT):
                    h_out(1, 1, d)

            def ffn_body(f, c, gate=None):
                base, q0, m0 = ((0, 0, 0), (FFN2_0, CHUNK_FFN2, PROD_FFN2))[f]
                split_unit(unit(base, c, 2))
                split_unit(unit(base, c, 3))
                product_hi(m0 + 2 * c, 0, q0 + c, unit(base, c, 1))
                silu_gate(unit(base, c, 2))
                split_unit(unit(base, c, 4))
                if gate == 0:
                    product_hi(m0 + 2 * c + 1, 1, q0 + c, unit(base, c, 3))
                    gate_out(gate)
                    split_unit(unit(base, c, 5))
                    split_down(q0 + c)
                else:
                    if gate is not None:
                        gate_out(gate)
                    split_down(q0 + c)
                    split_unit(unit(base, c, 5))
                    product_hi(m0 + 2 * c + 1, 1, q0 + c, unit(base, c, 3))
                silu_gate(unit(base, c, 4))

            def gate_out(stage):
                act.wait_ge(s_gatemm, stage + 1)
                q = (0, CHUNK_MIX, CHUNK_FFN2)[stage]
                if q:
                    act.wait_ge(s_dgate, 2 * q)
                act.activation(gate_row, flat(ps_down[0]), ACT.Copy).then_inc(s_gate, 1)

            def rope_sines():
                act.wait_ge(s_rt, ROPE_STEPS)
                act.activation(rope_w[:, 2, :], rope_w[:, 2, :], ACT.Sin).then_inc(s_sin, 1)
                act.activation(rope_w[:, 3, :], rope_w[:, 3, :], ACT.Sin).then_inc(s_sin, 1)

            for dst, src in const_loads[1::2]:
                act.dma_start(dst, src).then_inc(s_const, 16)
            for dst, src in ((ones[:], t["ones"][:, :]), (mask[:], t["mask"][:, :]),
                             (rope_c[:], t["rope_c"][:, :])):
                act.dma_start(dst, src).then_inc(s_ones, 16)
            act.wait_ge(s_cols, 1)
            act.activation(cond[:], cols[:, COL_C:COL_C + KT], ACT.Silu).then_inc(s_cond, 1)
            split_unit(unit(0, 0, 0))
            for d in range(KT):
                h_out(0, 0, d)
            split_unit(unit(0, 0, 1))
            for d in range(KT):
                h_out(0, 1, d)
            h_taken(0)
            silu_gate(unit(0, 0, 0))
            ffn_body(0, 0, gate=0)
            with act.Fori(1, FC - 1) as c:
                ffn_body(0, c)
            last_chunk(0)

            def copy_out(dst, u):
                n, before, par = u
                act.wait_ge(s_unit, n + 1)
                act.activation(dst, flat(ps_unit[par]), ACT.Copy).then_inc(s_pfree[par], 1)

            def swap_rotary(src, r):
                act.wait_ge(s_zero, 1)
                if r > 0:
                    act.wait_ge(s_rope, r)
                for b in (0, 64):
                    act.dma_start(q_swap[b:b + 8, :], src[b + 8:b + 16, :]).then_inc(s_swap, 16)
                    act.dma_start(q_swap[b + 8:b + 16, :], src[b:b + 8, :]).then_inc(s_swap, 16)

            split_unit(unit(MIX0, 0, 2))
            h_taken(1)
            copy_out(k_t, unit(MIX0, 0, 0))
            act.wait_ge(s_pfree[0], MIX0 // 2 + 1)
            swap_rotary(k_t, 0)
            split_unit(unit(MIX0, 0, 3))
            copy_out(q_t, unit(MIX0, 0, 1))
            act.wait_ge(s_pfree[1], MIX0 // 2 + 1)
            swap_rotary(q_t, 1)
            gate_out(1)
            copy_out(sg, unit(MIX0, 0, 2))

            def exps(j, b):
                n = TT * j + b
                k0 = 0 if b else P
                act.wait_ge(s_max, n + 1)
                for h in range(2):
                    act.activation(scores[:, b % 2, h, k0:], scores[:, b % 2, h, k0:], ACT.Exp,
                                   bias=at_s[:, b % 2, 2 + h:3 + h],
                                   accum_out=at_s[:, b % 2, 6 + h:7 + h])
                act.activation(at_s[:, b % 2, 8:10], at_s[:, b % 2, 4:6], ACT.Exp).then_inc(s_exp, 1)

            def probsT_out(j, b):
                n = TT * j + b
                act.wait_ge(s_pT, n + 1)
                if n >= 2:
                    act.wait_ge(s_pv, n - 1)
                k0 = 0 if b else 1
                act.activation(probsT[:, b % 2, k0:], ps_probsT[:, k0:], ACT.Copy).then_inc(s_pTc, 1)

            def attn_hi(j, g):
                act.wait_ge(s_pv, TT * j + 4 * g + 4)
                act.wait_ge(s_down, 8 * (CHUNK_MIX + j))
                act.activation(act_hi[:, 0, HALF * g:HALF * (g + 1)], ps_attn, ACT.Copy).then_inc(s_ahi, 1)

            split_unit(unit(MIX0, 0, 4))
            split_down(CHUNK_MIX)
            for j in range(PAIRS):
                last = j + 1 == PAIRS
                exps(j, 0)
                if j == 0:
                    act.wait_ge(s_vT, 1)
                    act.activation(v_tok, flat(ps_unit[0]), ACT.Copy).then_inc(s_v, 1)
                probsT_out(j, 0)
                exps(j, 1)
                probsT_out(j, 1)
                exps(j, 2)
                if j > 0:
                    act.wait_ge(s_conv, 3 * j)
                copy_out(sg, unit(MIX0, j, 3))
                probsT_out(j, 2)
                exps(j, 3)
                split_unit(unit(MIX0, j, 5))
                probsT_out(j, 3)
                exps(j, 4)
                attn_hi(j, 0)
                probsT_out(j, 4)
                split_unit(unit(MIX0, j, 6) if not last else unit(FFN2_0, 0, 0))
                for b in (5, 6, 7):
                    exps(j, b)
                    probsT_out(j, b)
                product_hi(PROD_MIX + j, 1, CHUNK_MIX + j, unit(MIX0, j, 5))
                attn_hi(j, 1)
                split_unit(unit(MIX0, j, 7) if not last else unit(FFN2_0, 0, 1))
                if not last:
                    copy_out(q_t, unit(MIX0, j, 6))
                    act.wait_ge(s_pfree[0], MIX0 // 2 + 4 + 2 * j)
                    swap_rotary(q_t, 2 + j)
                    split_unit(unit(MIX0, j + 1, 4))
                    split_down(CHUNK_MIX + j + 1)
            deviation(1, 0)
            for n in range(TT - 1):
                if n + 1 < TT - 1:
                    deviation(1, n + 1)
                normalise(1, n)
                for d in {4: (0, 1, 2), 5: (3, 4, 5, 6, 7)}.get(n, ()):
                    h_out(2, 0, d)
            deviation(1, TT - 1)
            normalise(1, TT - 1)
            for d in range(KT):
                h_out(2, 1, d)

            h_taken(2)
            silu_gate(unit(FFN2_0, 0, 0))
            ffn_body(1, 0, gate=2)
            with act.Fori(1, FC - 1) as c:
                ffn_body(1, c)
            last_chunk(1)

        @block.vector
        def _(dve):
            def split_unit(u):
                n, before, par = u
                dve.wait_ge(s_whi, n + 1)
                dve.tensor_tensor(wu_lo[:, par, :], raw_unit[:, par, :], wu_hi[:, par, :].bitcast(F32),
                                  ALU.subtract).then_inc(s_wlo, 1)

            def split_down(q, tiles=(0, 1)):
                for i in tiles:
                    dve.wait_ge(s_dhi, 2 * q + i + 1)
                    dve.tensor_tensor(wd_lo[:, i, :], raw_down[:, i, :], wd_hi[:, i, :].bitcast(F32),
                                      ALU.subtract).then_inc(s_dlo, 1)

            def glu(u, m, i, q):
                n, before, par = u
                dve.wait_ge(s_unit, n + 1)
                dve.wait_ge(s_pfree[0], before + 1)
                if not (isinstance(q, int) and q == 0 and i == 0):
                    dve.wait_ge(s_act[1 - i], 2 * q + 2 * i)
                product_halves(sg, par)

            def product_halves(x, par):
                for g, signal in enumerate((s_prod, s_pfree[par])):
                    at = slice(HALF * g, HALF * g + HALF)
                    dve.tensor_tensor(prod[:, at], x[:, at], ps_unit[par][:, g, :], ALU.mult
                                      ).then_inc(signal, 1)

            def last_glu(f, g):
                base, q = ((0, FC - 1), (FFN2_0, CHUNK_FFN2 + FC - 1))[f]
                n, before, par = unit(base, FC - 1, 3)
                if g == 0:
                    dve.wait_ge(s_uhalf, 2 * f + 2)
                    dve.wait_ge(s_silu, f + 1)
                    dve.wait_ge(s_act[0], 2 * q + 2)
                else:
                    dve.wait_ge(s_unit, n + 1)
                    dve.wait_ge(s_pfree[0], before + 1)
                at = slice(HALF * g, HALF * g + HALF)
                dve.tensor_tensor(prod[:, at], sg[:, at], ps_unit[par][:, g, :], ALU.mult
                                  ).then_inc((s_prod, s_pfree[par])[g], 1)

            def product_lo(m, i, halves=(0, 1)):
                for g in halves:
                    at = slice(HALF * g, HALF * g + HALF)
                    dve.wait_ge(s_phi, 2 * m + g + 1)
                    dve.tensor_tensor(act_lo[:, i, at], prod[:, at], act_hi[:, i, at].bitcast(F32),
                                      ALU.subtract).then_inc(s_act[i], 1)

            def strip_products(n, k_tiles=range(KT)):
                for k in k_tiles:
                    part = strip_part(n, k // 4)[:, k % 4, :]
                    if k % 4 == 0:
                        if is_early(n):
                            dve.wait_ge(s_strip_early[n][k // 4], 16)
                        else:
                            dve.wait_ge(s_strip[k // 4], 16 if isinstance(n, int) and n == 0 else 16 * (n - 1))
                    acc = acc_of(n)
                    if k == 0:
                        two = isinstance(n, int) and n <= STRIPS_BEFORE
                        if not (two and n < 2):
                            dve.wait_ge(s_modmm, n - 1 if two else n)
                        dve.tensor_scalar(acc, part, cond[:, 0:1], None, ALU.mult
                                          ).then_inc(s_acc, 1)
                        continue
                    dve.wait_ge(s_acc, 8 * n + k)
                    dve.scalar_tensor_tensor(acc, part, cond[:, k:k + 1], acc,
                                             ALU.mult, ALU.add).then_inc(s_acc, 1)

            def mod_out(n):
                dve.wait_ge(s_modmm, n + 1)
                dve.tensor_reduce(mod_sum[:], ps_mod.rearrange("p (i k) -> p i k", k=P), AXX, ALU.add
                                  ).then_inc(s_modsum, 1)
                dve.wait_ge(s_modsum, n + 1)
                dve.tensor_tensor(mod[:, bass.ds(4 * n, 4)], mod_sum[:], cols[:, bass.ds(COL_BADA + 4 * n, 4)],
                                  ALU.add).then_inc(s_mod, 1)

            def affine_cols(stage):
                sh, sc = mod[:, 24 * stage:24 * stage + 8], mod[:, 24 * stage + 8:24 * stage + 16]
                a, b = affine[:, stage, 0, :], affine[:, stage, 1, :]
                if stage == 0:
                    dve.tensor_scalar(a, sc, 1.0, None, ALU.add).then_inc(s_ln, 1)
                    dve.tensor_scalar(b, sh, 0.0, None, ALU.add).then_inc(s_ln, 1)
                    dve.wait_ge(s_ln, steps(2))
                    dve.nop().then_inc(s_aff, 1)
                    return
                g = cols[:, COL_LN + 16 * (stage - 1):COL_LN + 16 * (stage - 1) + 8]
                lb = cols[:, COL_LN + 16 * (stage - 1) + 8:COL_LN + 16 * stage]
                dve.scalar_tensor_tensor(a, sc, 1.0, g, ALU.add, ALU.mult).then_inc(s_ln, 1)
                dve.scalar_tensor_tensor(b, sc, 1.0, lb, ALU.add, ALU.mult).then_inc(s_ln, 1)
                dve.wait_ge(s_ln, steps(2))
                dve.tensor_tensor(b, b, sh, ALU.add).then_inc(s_aff, 1)

            ln_count = [0]

            def steps(n):
                ln_count[0] += n
                return ln_count[0]

            def gate_diagonal(stage):
                g = mod[:, 24 * stage + 16:24 * stage + 24]
                factor = (0.5, 1.0, 0.5)[stage]
                dve.tensor_scalar(gate_c[:], g, 1.0, factor, ALU.add, ALU.mult).then_inc(s_ln, 1)
                dve.wait_ge(s_ln, steps(1))
                await_stage_h(dve, stage)
                for d in range(KT):
                    ins = dve.tensor_scalar(diag[:, P * d:P * d + P], ident[:], gate_c[:, d:d + 1], None,
                                            ALU.mult)
                ins.then_inc(s_diag, 1)

            def h_split(n):
                d, at = n % KT, slice(HALF * (n // KT % 2), HALF * (n // KT % 2) + HALF)
                dve.wait_ge(s_ev, n + 1)
                dve.tensor_copy(h_hi[:, d, at], h_tmp[n % 4]).then_inc(s_hhi, 1)
                if not pool_splits(n):
                    dve.wait_ge(s_hhi, n + 1)
                    dve.tensor_tensor(h_lo[:, d, at], h_tmp[n % 4], h_hi[:, d, at].bitcast(F32),
                                      ALU.subtract).then_inc(s_h, 1)

            def add_y(q, n, stage=None):
                dve.wait_ge(s_down, 8 * q + n + 1)
                if stage is not None:
                    await_residual(stage, n)
                elif not (isinstance(q, int) and q == 0):
                    dve.wait_ge(s_y, 8 * q + n - 7)
                dve.tensor_tensor(y[:, n, :], y[:, n, :], flat(ps_down[n % 2]), ALU.add).then_inc(s_y, 1)

            def residual(stage, n):
                dve.wait_ge(s_tr, 16 * stage + 8 * (n // 4) + 8)
                if stage == 0:
                    dve.tensor_scalar(y[:, n, :], y[:, n, :], ALPHA, None, ALU.mult).then_inc(s_resd, 1)
                    return
                dve.tensor_tensor(y[:, n, :], y[:, n, :], ln_g_row, ALU.mult).then_inc(s_rmd, 1)
                dve.wait_ge(s_rmd, 4 * (stage - 1) + n // 2 + 1)
                dve.tensor_tensor(y[:, n, :], y[:, n, :], ln_b_row, ALU.add).then_inc(s_resd, 1)

            def await_residual(stage, n):
                if stage == 0:
                    dve.wait_ge(s_resd, n + 1)
                elif n % 2:
                    dve.wait_ge(s_resd, TT + 4 * (stage - 1) + n // 2 + 1)
                else:
                    dve.wait_ge(s_res, 4 * (stage - 1) + n // 2 + 1)

            def scale_rows(stage):
                dve.wait_ge(s_rows, 32 * stage)
                for row in (ln_g_row, ln_b_row):
                    dve.tensor_scalar(row, row, ALPHA, None, ALU.mult).then_inc(s_rowsc, 1)
                dve.wait_ge(s_rowsc, 2 * stage)

            def invert(ln, n):
                dve.wait_ge(s_std, TT * ln + n + 1)
                dve.reciprocal(ln_s[:, n % 4, 16:17], ln_s[:, n % 4, 15:16]).then_inc(s_rcp, 1)

            def statistics(ln, q, n):
                s = ln_s[:, n % 4, :]
                m = TT * ln + n
                add_y(q, n)
                if n > 0 and n != (4, 7, 4)[ln]:
                    invert(ln, n - 1)
                if ln == 2 and n >= 4:
                    if n - 4 in OUT_VECTOR:
                        dve.wait_ge(s_on, OUT_VECTOR.index(n - 4) + 1)
                    else:
                        dve.wait_ge(s_norm, 2 * TT + OUT_POOL.index(n - 4) + 1)
                elif m >= 4:
                    dve.wait_ge(s_norm, m - 3)
                dve.wait_ge(s_y, 8 * q + n + 1)
                for i in range(2):
                    dve.bn_stats(s[:, 6 * i:6 * i + 6], y[:, n, HALF * i:HALF * i + HALF]).then_inc(s_ln, 1)
                dve.wait_ge(s_ln, steps(2))
                dve.bn_aggr(s[:, 12:14], s[:, 0:12]).then_inc(s_var, 1)

            def ln_turn(stage, q):
                ln = stage - 1
                for n in range(TT - 1):
                    statistics(ln, q, n)
                h_split(16 * stage)
                h_split(16 * stage + 1)
                invert(ln, TT - 2)
                for i in range(2, KT):
                    h_split(16 * stage + i)
                statistics(ln, q, TT - 1)
                invert(ln, TT - 1)
                for i in range(KT, 2 * KT):
                    h_split(16 * stage + i)

            def last_chunk(f):
                base, q, m = ((0, FC - 1, PROD_MIX - 1), (FFN2_0, CHUNK_FFN2 + FC - 1, PROD_FFN2 + 2 * FC - 1))[f]
                ln = 2 * f
                split_unit(unit(base, FC - 1, 2))
                if f == 0:
                    rope_angles()
                    strip_products(STRIPS - 1)
                glu(unit(base, FC - 1, 1), m - 1, 0, q)
                split_unit(unit(base, FC - 1, 3))
                product_lo(m - 1, 0)
                split_down(q)
                if f == 0:
                    mod_out(STRIPS - 1)
                    dve.wait_ge(s_mod, STRIPS)
                    affine_cols(1)
                    affine_cols(2)
                    dve.wait_ge(s_sin, 1)
                    dve.tensor_scalar(rope_w[:, 4, :], rope_w[:, 2, :], -1.0, None, ALU.mult).then_inc(s_rtab, 1)
                last_glu(f, 0)
                product_lo(m, 1, (0,))
                for n in range(4):
                    statistics(ln, q, n)
                if f:
                    dve.wait_ge(s_ow, 64)
                    gained(0)
                    invert(ln, 3)
                    gained(1)
                    out_affine(0)
                    out_affine(1)
                    last_glu(f, 1)
                    product_lo(m, 1, (1,))
                    for n in range(4, TT):
                        statistics(ln, q, n)
                    gained(5)
                    invert(ln, TT - 1)
                    out_affine(5)
                    for n in (6, 7):
                        gained(n)
                        out_affine(n)
                    return
                invert(ln, 3)
                scale_rows(1)
                split_unit(unit(base, FC, 0))
                h_split(16)
                h_split(17)
                last_glu(f, 1)
                h_split(18)
                product_lo(m, 1, (1,))
                h_split(19)
                h_split(20)
                statistics(ln, q, 4)
                h_split(21)
                statistics(ln, q, 5)
                h_split(22)
                h_split(23)
                split_unit(unit(base, FC, 1))
                statistics(ln, q, 6)
                statistics(ln, q, 7)
                invert(ln, 7)
                residual(1, 1)
                for d in range(KT):
                    h_split(16 + KT + d)

            def gained(n):
                dve.wait_ge(s_var, 2 * TT + n + 1)
                dve.scalar_tensor_tensor(y[:, n, :], y[:, n, :], ln_s[:, n % 4, 12:13], out_g_row,
                                         ALU.subtract, ALU.mult).then_inc(s_og, 1)

            def out_affine(n):
                dve.wait_ge(s_stat, 2 * TT + n + 1)
                dve.wait_ge(s_og, OUT_VECTOR.index(n) + 1)
                dve.scalar_tensor_tensor(y[:, n, :], y[:, n, :], ln_s[:, n % 4, 20:21], out_b_row,
                                         ALU.mult, ALU.add).then_inc(s_on, 1)

            def ffn_body(f, c, strip_n=None, first=False):
                base, q0, m0 = ((0, 0, 0), (FFN2_0, CHUNK_FFN2, PROD_FFN2))[f]
                split_unit(unit(base, c, 2))
                glu(unit(base, c, 1), m0 + 2 * c, 0, q0 + c)
                product_lo(m0 + 2 * c, 0)
                split_unit(unit(base, c, 3))
                if first and f:
                    for n in range(1, TT, 2):
                        residual(2, n)
                if first and not f:
                    gate_of_ffn1()
                    glu(unit(base, c, 3), m0 + 2 * c + 1, 1, q0 + c)
                    product_lo(m0 + 2 * c + 1, 1)
                    strip_products(6)
                    split_unit(unit(base, c, 5))
                    split_down(q0 + c)
                    mod_out(6)
                else:
                    if strip_n is not None:
                        strip_products(strip_n)
                    split_unit(unit(base, c, 4))
                    split_down(q0 + c)
                    glu(unit(base, c, 3), m0 + 2 * c + 1, 1, q0 + c)
                    product_lo(m0 + 2 * c + 1, 1)
                    split_unit(unit(base, c, 5))
                    if strip_n is not None:
                        mod_out(strip_n)
                for n in range(TT):
                    add_y(q0 + c, n, 2 * f if first else None)
                    if strip_n is not None and first:
                        strip_products(strip_n, (n,))
                if strip_n is not None and first:
                    mod_out(strip_n)

            def gate_of_ffn1():
                strip_products(4)
                split_unit(unit(0, 0, 4))
                mod_out(4)
                strip_products(5)
                mod_out(5)
                dve.wait_ge(s_mod, 6)
                gate_diagonal(0)

            dve.memset(eps[:], LN_EPS).then_inc(s_eps, 1)
            dve.wait_ge(s_colsT, 1)
            dve.tensor_copy(cols[:], ps_unit[0][:, 0, 0:N_COLS]).then_inc(s_cols, 1)
            dve.wait_ge(s_cond, 1)
            strip_products(0)
            strip_products(1)
            for n in range(2, 4):
                mod_out(n - 2)
                strip_products(n)
            mod_out(2)
            split_unit(unit(0, 0, 0))
            mod_out(3)
            dve.wait_ge(s_mod, 4)
            affine_cols(0)
            for n in range(2 * KT):
                if n == KT:
                    split_unit(unit(0, 0, 1))
                h_split(n)
            for n in range(TT):
                residual(0, n)

            def rope_angles():
                done = [0]
                pos, tmp, ang, turns = (rope_w[:, i, :] for i in (0, 1, 3, 2))

                def step(ins):
                    ins.then_inc(s_rt, 1)
                    done[0] += 1
                    dve.wait_ge(s_rt, done[0])
                dve.wait_ge(s_pos, 16 * (ROT // 2))
                step(dve.tensor_copy(tmp, pos.bitcast(I32)))
                step(dve.tensor_scalar(ang, tmp, rope_c[:, 0:1], None, ALU.mult))
                step(dve.tensor_scalar(turns, ang, 1.0 / (2 * PI), None, ALU.mult))
                step(dve.tensor_scalar(turns, turns, ROUND_1, None, ALU.add))
                step(dve.tensor_scalar(turns, turns, -ROUND_1, None, ALU.add))
                step(dve.tensor_scalar(tmp, turns, ROUND_2K, None, ALU.add))
                step(dve.tensor_scalar(tmp, tmp, -ROUND_2K, None, ALU.add))
                step(dve.tensor_tensor(turns, turns, tmp, ALU.subtract))
                for part in (TWO_PI_1, TWO_PI_2, TWO_PI_3):
                    for n in (tmp, turns):
                        step(dve.scalar_tensor_tensor(ang, n, -part, ang, ALU.mult, ALU.add))
                step(dve.tensor_scalar(turns, ang, PI, -PI, ALU.min, ALU.max))
                step(dve.tensor_scalar(ang, ang, PI / 2, None, ALU.add))
                step(dve.tensor_scalar(tmp, ang, PI, -2 * PI, ALU.is_gt, ALU.mult))
                step(dve.tensor_tensor(ang, ang, tmp, ALU.add))
                step(dve.tensor_scalar(ang, ang, PI, -PI, ALU.min, ALU.max))
                assert done[0] == ROPE_STEPS

            ffn_body(0, 0, 7, first=True)
            with dve.Fori(1, FC - 1) as c:
                ffn_body(0, c, STRIPS_BEFORE + c)
            last_chunk(0)

            gate_diagonal(1)
            split_unit(unit(MIX0, 0, 2))

            def rope(dst, r, adds=()):
                dve.wait_ge(s_swap, 64 * (r + 1))
                dve.tensor_tensor(q_swap, q_swap, sin_t, ALU.mult).then_inc(s_rs, 1)
                for add in adds[0:1]:
                    add()
                dve.tensor_tensor(dst, dst, cos_t, ALU.mult).then_inc(s_rs, 1)
                for add in adds[1:2]:
                    add()
                dve.wait_ge(s_rs, 2 * (r + 1))
                dve.tensor_tensor(dst, dst, q_swap, ALU.add).then_inc(s_rope, 1)

            dve.wait_ge(s_rload, 128)
            residual(1, 3)
            rope(k_t, 0)
            split_unit(unit(MIX0, 0, 3))
            rope(q_t, 1)
            residual(1, 5)
            residual(1, 7)
            split_unit(unit(MIX0, 0, 4))
            dve.wait_ge(s_res, 4)
            dve.wait_ge(s_sink, 16)
            dve.tensor_scalar(neg_sink[:], sink[:], -1.0, None, ALU.mult).then_inc(s_nsink, 1)
            dve.wait_ge(s_nsink, 1)
            sm = [0]

            def sm_step():
                sm[0] += 1
                return sm[0]

            def softmax_max(j, b):
                n = TT * j + b
                k0 = 0 if b else P
                s = at_s[:, b % 2, :]
                dve.wait_ge(s_sc, n + 1)
                if n >= 2:
                    dve.wait_ge(s_pT, n - 1)
                sc = scores[:, b % 2, :, k0:]
                ps = ps_score[:, :, 256 * (b % 2) + k0:256 * (b % 2) + 256]
                mk = mask[:, k0:].unsqueeze(1).to_broadcast([P, 2, 2 * P - k0])
                dve.scalar_tensor_tensor(sc, ps, SCALE, mk, ALU.mult, ALU.add).then_inc(s_msk, 1)
                dve.wait_ge(s_msk, n + 1)
                dve.tensor_reduce(s[:, 0:2], sc, AXX, ALU.max).then_inc(s_sm, 1)
                dve.wait_ge(s_sm, sm_step())
                dve.scalar_tensor_tensor(s[:, 2:4], s[:, 0:2], -1.0, neg_sink[:, :, j], ALU.mult, ALU.min
                                         ).then_inc(s_sm, 1)
                dve.wait_ge(s_sm, sm_step())
                dve.tensor_tensor(s[:, 4:6], sink[:, :, j], s[:, 2:4], ALU.add).then_inc(s_max, 1)

            def softmax_norm(j, b):
                n = TT * j + b
                k0 = 0 if b else P
                s = at_s[:, b % 2, :]
                dve.wait_ge(s_exp, n + 1)
                dve.tensor_tensor(s[:, 10:12], s[:, 6:8], s[:, 8:10], ALU.add).then_inc(s_sm, 1)
                dve.wait_ge(s_sm, sm_step())
                dve.reciprocal(s[:, 12:14], s[:, 10:12]).then_inc(s_sm, 1)
                dve.wait_ge(s_sm, sm_step())
                sc = scores[:, b % 2, :, k0:]
                dve.tensor_tensor(sc, sc, s[:, 12:14].unsqueeze(2).to_broadcast([P, 2, 2 * P - k0]),
                                  ALU.mult).then_inc(s_p, 1)

            def attn_lo(j, g):
                dve.wait_ge(s_ahi, 2 * j + g + 1)
                at = slice(HALF * g, HALF * g + HALF)
                dve.tensor_tensor(act_lo[:, 0, at], ps_attn, act_hi[:, 0, at].bitcast(F32), ALU.subtract
                                  ).then_inc(s_act[0], 1)

            def conv(j):
                w = [cols[:, COL_CONV + 4 * tap + j:COL_CONV + 4 * tap + j + 1] for tap in range(3)]
                dve.wait_ge(s_unit, MIX0 + 4 * j + 5)
                dve.wait_ge(s_pfree[1], MIX0 // 2 + 2 * j + 2)
                dve.tensor_tensor(sg, sg, flat(ps_unit[0]), ALU.mult).then_inc(s_pfree[0], 1)
                yield
                dve.wait_ge(s_pfree[0], MIX0 // 2 + 2 * j + 3)
                dve.wait_ge(s_act[1], 2 * (CHUNK_MIX + j))
                dve.tensor_scalar(prod, sg, w[2], None, ALU.mult).then_inc(s_conv, 1)
                yield
                for tap in (1, 0):
                    lag = 2 - tap
                    dve.wait_ge(s_conv, 3 * j + lag)
                    dve.scalar_tensor_tensor(prod[:, lag:], sg[:, 0:SEQ - lag], w[tap], prod[:, lag:],
                                             ALU.mult, ALU.add).then_inc(s_conv, 1)
                    yield

            def conv_gate(j):
                dve.wait_ge(s_unit, MIX0 + 4 * j + 6)
                dve.wait_ge(s_conv, 3 * j + 3)
                product_halves(prod, 1)

            for j in range(PAIRS):
                last = j + 1 == PAIRS
                taps = conv(j)
                for b in range(4):
                    softmax_max(j, b)
                    softmax_norm(j, b)
                    if j == 0 and b < 2:
                        split_down(CHUNK_MIX, (b,))
                split_unit(unit(MIX0, j, 5))
                softmax_max(j, 4)
                attn_lo(j, 0)
                softmax_norm(j, 4)
                softmax_max(j, 5)
                split_unit(unit(MIX0, j, 6) if not last else unit(FFN2_0, 0, 0))
                softmax_norm(j, 5)
                next(taps)
                softmax_max(j, 6)
                next(taps)
                softmax_norm(j, 6)
                next(taps)
                softmax_max(j, 7)
                next(taps)
                softmax_norm(j, 7)
                conv_gate(j)
                product_lo(PROD_MIX + j, 1)
                attn_lo(j, 1)
                split_unit(unit(MIX0, j, 7) if not last else unit(FFN2_0, 0, 1))
                if not last:
                    q, stage = CHUNK_MIX + j, 1 if j == 0 else None
                    for n in range(3):
                        add_y(q, n, stage)
                    rope(q_t, 2 + j, [lambda n=n: add_y(q, n, stage) for n in (3, 4)])
                    add_y(q, 5, stage)
                    split_unit(unit(MIX0, j + 1, 4))
                    add_y(q, 6, stage)
                    add_y(q, 7, stage)
                    split_down(q + 1)
            ln_turn(2, CHUNK_MIX + PAIRS - 1)

            gate_diagonal(2)
            scale_rows(2)

            ffn_body(1, 0, first=True)
            with dve.Fori(1, FC - 1) as c:
                ffn_body(1, c)
            last_chunk(1)

        @block.gpsimd
        def _(pool):
            def gate_down(q):
                for i in range(2):
                    pool.wait_ge(s_rawd[i], 32 * q + 32)
                    pool.tensor_tensor(raw_down[:, i, :], raw_down[:, i, :], gate_row, ALU.mult
                                       ).then_inc(s_dgate, 1)

            def residual(stage, n):
                pool.wait_ge(s_tr, 16 * stage + 8 * (n // 4) + 8)
                pool.tensor_tensor(y[:, n, :], y[:, n, :], ln_g_row, ALU.mult).then_inc(s_rm, 1)
                pool.wait_ge(s_rm, 4 * (stage - 1) + n // 2 + 1)
                pool.tensor_tensor(y[:, n, :], y[:, n, :], ln_b_row, ALU.add).then_inc(s_res, 1)

            def row_scale(ln, n):
                s = ln_s[:, n % 4, :]
                m = TT * ln + n
                count = [4 * m]

                def step(ins):
                    ins.then_inc(s_newton, 1)
                    count[0] += 1
                    pool.wait_ge(s_newton, count[0])
                pool.wait_ge(s_var, m + 1)
                step(pool.tensor_scalar(s[:, 14:15], s[:, 13:14], LN_EPS, None, ALU.add))
                pool.wait_ge(s_rcp, m + 1)
                step(pool.tensor_scalar(s[:, 18:19], s[:, 16:17], s[:, 16:17], s[:, 14:15], ALU.mult, ALU.mult))
                step(pool.tensor_scalar(s[:, 19:20], s[:, 18:19], -0.5, 1.5, ALU.mult, ALU.add))
                step(pool.tensor_tensor(s[:, 20:21], s[:, 16:17], s[:, 19:20], ALU.mult))
                pool.tensor_scalar(s[:, 21:22], s[:, 20:21], s[:, 12:13], -1.0, ALU.mult, ALU.mult
                                   ).then_inc(s_stat, 1)

            def h_lo_part(stage, tiles=range(2 * KT)):
                for n in (16 * stage + i for i in tiles):
                    if pool_splits(n):
                        d, at = n % KT, slice(HALF * (n // KT % 2), HALF * (n // KT % 2) + HALF)
                        pool.wait_ge(s_hhi, n + 1)
                        pool.tensor_tensor(h_lo[:, d, at], h_tmp[n % 4], h_hi[:, d, at].bitcast(F32),
                                           ALU.subtract).then_inc(s_hp, 1)

            pool.wait_ge(s_acc, 8 * 3)
            pool.memset(cos_t, 1.0).then_inc(s_rbase, 1)
            pool.memset(sin_t, 0.0).then_inc(s_rbase, 1)
            h_lo_part(0)
            pool.wait_ge(s_gate, 1)
            gate_down(0)
            with pool.Fori(1, FC) as c:
                gate_down(c)
            for stage, q in ((1, CHUNK_MIX), (2, CHUNK_FFN2)):
                tile_after = ({3: 1, 4: 5}, {5: 1, 6: 5})[stage - 1]
                for n in range(TT):
                    row_scale(stage - 1, n)
                    if n in tile_after:
                        h_lo_part(stage, (tile_after[n],))
                if stage == 1:
                    pool.wait_ge(s_rowsc, 2)
                    pool.memset(q_swap, 0.0).then_inc(s_zero, 1)
                    residual(1, 0)
                h_lo_part(stage, range(max(tile_after.values()) + 1, 2 * KT))
                pool.wait_ge(s_rowsc, 2 * stage)
                for n in range(2 if stage == 1 else 0, TT, 2):
                    residual(stage, n)
                pool.wait_ge(s_gate, stage + 1)
                gate_down(q)
                if stage == 1:
                    for j in range(1, PAIRS):
                        gate_down(q + j)
            with pool.Fori(1, FC) as c:
                gate_down(CHUNK_FFN2 + c)

            def out_row(n):
                m = OUT_POOL.index(n)
                pool.wait_ge(s_norm, 2 * TT + m + 1)
                pool.tensor_tensor(y[:, n, :], y[:, n, :], out_g_row, ALU.mult).then_inc(s_ogp, 1)
                pool.wait_ge(s_ogp, m + 1)
                pool.tensor_tensor(y[:, n, :], y[:, n, :], out_b_row, ALU.add).then_inc(s_oa, 1)

            pool.wait_ge(s_ow, 64)
            for n in range(TT):
                row_scale(2, n)
                for done in {3: (2, 3), 4: (4,)}.get(n, ()):
                    out_row(done)


def constants():
    q, k = np.arange(P)[:, None], np.arange(2 * P)[None, :]
    lag = q + P - k
    mask = np.where((lag >= 0) & (lag < P), 0.0, MASKED).astype(np.float32)
    freq = THETA ** (-2.0 * (np.arange(P) // 16) / ROT)
    return {"ident": np.eye(P, dtype=np.float32), "ones": np.ones((P, P), np.float32), "mask": mask,
            "rope_c": freq[:, None].astype(np.float32)}


def kernel(**inputs):
    import concourse.bacc as bacc
    from concourse.bass_utils import run_bass_kernel_spmd

    nc = bacc.Bacc("TRN2", target_bir_lowering=False, num_devices=1)
    arrays = {}
    for name, a in inputs.items():
        a = np.ascontiguousarray(a)
        arrays[name] = a if name == "c" else a[0]
    arrays.update(constants())
    handles = {name: nc.dram_tensor(name + "_dram", a.shape, mybir.dt.from_np(a.dtype), kind="ExternalInput").ap()
               for name, a in arrays.items()}
    out = nc.dram_tensor("out_dram", (SEQ, D), F32, kind="ExternalOutput").ap()
    build(nc, handles, out)
    r = run_bass_kernel_spmd(nc, [{name + "_dram": a for name, a in arrays.items()}], core_ids=[0])
    return r.results[0]["out_dram"].reshape(1, SEQ, D)
```
